# Optimizing a Trainium2 kernel written in Bass

```python
import math
import jax, jax.numpy as jnp
from jax import lax
import numpy as np

D_MODEL = 1024
BATCH = 1
SEQ = 256
DEPTH = 1

GDN_HEADS = 8
GDN_DK = 128
GDN_DV = 128
GDN_CONV = 4
GDN_CHUNK = 64
MLA_HEADS = 8
MLA_Q_RANK = 384
MLA_KV_RANK = 256
MLA_NOPE = 128
MLA_ROPE = 64
MLA_V = 128
ROPE_THETA = 10000.0
Q_BLOCK = 128
D_FF = 2816
FFN_CONV = 3
EPS = 1e-6

SPLIT_SIZES = (
    3 * GDN_HEADS * GDN_DK if GDN_DK == GDN_DV else 2 * GDN_HEADS * GDN_DK + GDN_HEADS * GDN_DV,
    GDN_HEADS * GDN_DV,
    GDN_HEADS,
    GDN_HEADS,
    MLA_Q_RANK,
    MLA_KV_RANK,
    MLA_ROPE,
    D_MODEL,
    D_MODEL,
)
D_IN = sum(SPLIT_SIZES)


def rmsnorm(x, g):
    xf = x.astype(jnp.float32)
    xf = xf * lax.rsqrt(jnp.mean(xf * xf, axis=-1, keepdims=True) + EPS)
    return (xf * g.astype(jnp.float32)).astype(x.dtype)

def l2norm(x):
    return x * lax.rsqrt(jnp.sum(x * x, axis=-1, keepdims=True) + EPS)

def causal_dwconv(x, w):
    k = w.shape[0]
    return lax.conv_general_dilated(
        x, w[:, None, :].astype(x.dtype), window_strides=(1,), padding=[(k - 1, 0)],
        dimension_numbers=("NWC", "WIO", "NWC"), feature_group_count=x.shape[-1])

def split_in(z):
    offs = list(np.cumsum(SPLIT_SIZES)[:-1])
    return jnp.split(z, [int(o) for o in offs], axis=-1)

def rope(x, pos):
    half = x.shape[-1] // 2
    inv = ROPE_THETA ** (-jnp.arange(half, dtype=jnp.float32) / half)
    ang = pos.astype(jnp.float32)[:, None] * inv[None, :]
    cos = jnp.cos(ang)[:, None, :]
    sin = jnp.sin(ang)[:, None, :]
    xf = x.astype(jnp.float32)
    x1, x2 = xf[..., :half], xf[..., half:]
    return jnp.concatenate([x1 * cos - x2 * sin, x2 * cos + x1 * sin], axis=-1).astype(x.dtype)

def gdn_chunked(q, k, v, g, beta):
    b, s, h, dk = q.shape
    dv = v.shape[-1]
    c = GDN_CHUNK
    n = s // c
    f32 = jnp.float32
    q = l2norm(q.astype(f32)) * (dk ** -0.5)
    k = l2norm(k.astype(f32))
    v = v.astype(f32)

    def chunk(t):
        t = t.reshape((b, n, c, h) + t.shape[3:])
        return jnp.moveaxis(t, 3, 1)

    q, k, v = chunk(q), chunk(k), chunk(v)
    g = jnp.cumsum(chunk(g.astype(f32)), axis=-1)
    beta = chunk(beta.astype(f32))
    k_beta = k * beta[..., None]
    v_beta = v * beta[..., None]

    causal = jnp.tril(jnp.ones((c, c), dtype=bool))
    diff = g[..., :, None] - g[..., None, :]
    decay = jnp.where(causal, jnp.exp(jnp.where(causal, diff, 0.0)), 0.0)

    lmat = jnp.einsum("bhnid,bhnjd->bhnij", k_beta, k) * decay
    rhs = jnp.concatenate([v_beta, k_beta * jnp.exp(g)[..., None]], axis=-1)
    sol = lax.linalg.triangular_solve(lmat, rhs, left_side=True, lower=True, unit_diagonal=True)
    u, w = sol[..., :dv], sol[..., dv:]

    a_intra = jnp.einsum("bhnid,bhnjd->bhnij", q, k) * decay
    q_dec = q * jnp.exp(g)[..., None]
    k_dec = k * jnp.exp(g[..., -1:] - g)[..., None]
    g_last = jnp.exp(g[..., -1])

    xs = tuple(jnp.moveaxis(t, 2, 0) for t in (u, w, q_dec, k_dec, a_intra, g_last))

    def step(state, inp):
        u_n, w_n, qd_n, kd_n, a_n, gl_n = inp
        v_new = u_n - jnp.einsum("bhck,bhkv->bhcv", w_n, state)
        o = jnp.einsum("bhck,bhkv->bhcv", qd_n, state) + jnp.einsum("bhij,bhjv->bhiv", a_n, v_new)
        state = state * gl_n[..., None, None] + jnp.einsum("bhck,bhcv->bhkv", kd_n, v_new)
        return state, o

    s0 = jnp.zeros((b, h, dk, dv), dtype=f32)
    _, o = lax.scan(step, s0, xs)
    o = jnp.transpose(o, (1, 0, 3, 2, 4)).reshape(b, s, h, dv)
    return o

def mla_causal(q_nope, q_pe, k_nope, k_pe, v):
    s = q_nope.shape[1]
    scale = (MLA_NOPE + MLA_ROPE) ** -0.5
    outs = []
    for i in range(s // Q_BLOCK):
        q0, q1 = i * Q_BLOCK, (i + 1) * Q_BLOCK
        sc = (jnp.einsum("bqhd,bkhd->bhqk", q_nope[:, q0:q1], k_nope[:, :q1])
              + jnp.einsum("bqhr,bkr->bhqk", q_pe[:, q0:q1], k_pe[:, :q1]))
        sc = sc.astype(jnp.float32) * scale
        qpos = q0 + jnp.arange(Q_BLOCK)
        kpos = jnp.arange(q1)
        sc = jnp.where(qpos[:, None] >= kpos[None, :], sc, -jnp.inf)
        p = jax.nn.softmax(sc, axis=-1).astype(v.dtype)
        outs.append(jnp.einsum("bhqk,bkhd->bqhd", p, v[:, :q1]))
    return jnp.concatenate(outs, axis=1)

def first_inputs(seed: int = 0) -> dict:
    key = jax.random.key(seed)
    ks = jax.random.split(key, 24)
    L, D = DEPTH, D_MODEL
    nrm = lambda k, shape, fan: jax.random.normal(k, shape, jnp.float32) * (fan ** -0.5)
    gain = lambda k, n: 1.0 + 0.05 * jax.random.normal(k, (L, n), jnp.float32)
    a_log = jnp.log(jax.random.uniform(ks[3], (L, GDN_HEADS), jnp.float32, 1.0, 16.0))
    dt = jnp.exp(jax.random.uniform(ks[4], (L, GDN_HEADS), jnp.float32, math.log(1e-3), math.log(1e-1)))
    dt_bias = dt + jnp.log(-jnp.expm1(-dt))
    return {
        "x": jax.random.normal(ks[0], (BATCH, SEQ, D), jnp.float32),
        "norm_mix_g": gain(ks[1], D),
        "w_in": nrm(ks[2], (L, D, D_IN), D),
        "conv_qkv_w": nrm(ks[5], (L, GDN_CONV, SPLIT_SIZES[0]), GDN_CONV),
        "gdn_a_log": a_log,
        "gdn_dt_bias": dt_bias,
        "gdn_norm_g": gain(ks[6], GDN_DV),
        "mla_q_norm_g": gain(ks[7], MLA_Q_RANK),
        "w_uq": nrm(ks[8], (L, MLA_Q_RANK, MLA_HEADS * (MLA_NOPE + MLA_ROPE)), MLA_Q_RANK),
        "mla_kv_norm_g": gain(ks[9], MLA_KV_RANK),
        "w_ukv": nrm(ks[10], (L, MLA_KV_RANK, MLA_HEADS * (MLA_NOPE + MLA_V)), MLA_KV_RANK),
        "w_o_gdn": nrm(ks[11], (L, GDN_HEADS * GDN_DV, D), GDN_HEADS * GDN_DV),
        "w_o_mla": nrm(ks[12], (L, MLA_HEADS * MLA_V, D), MLA_HEADS * MLA_V),
        "w_out": nrm(ks[13], (L, D, D), D),
        "norm_ffn_g": gain(ks[14], D),
        "w_up": nrm(ks[15], (L, D, 2 * D_FF), D),
        "conv_ffn_w": nrm(ks[16], (L, FFN_CONV, 2 * D_FF), FFN_CONV),
        "w_down": nrm(ks[17], (L, D_FF, D), D_FF),
        "norm_final_g": 1.0 + 0.05 * jax.random.normal(ks[18], (D,), jnp.float32),
    }

def first_block(x, norm_mix_g, w_in, conv_qkv_w, gdn_a_log, gdn_dt_bias, gdn_norm_g,
              mla_q_norm_g, w_uq, mla_kv_norm_g, w_ukv, w_o_gdn, w_o_mla, w_out,
              norm_ffn_g, w_up, conv_ffn_w, w_down, norm_final_g):
    b, s, _ = x.shape
    pos = jnp.arange(s)
    hA, hB = GDN_HEADS, MLA_HEADS
    for l in range(DEPTH):
        h = rmsnorm(x, norm_mix_g[l])
        z = jnp.einsum("bsd,de->bse", h, w_in[l])
        qkv_a, gate_a, a_a, b_a, c_q, c_kv, k_pe, gate_br_a, gate_br_b = split_in(z)

        qkv_a = jax.nn.silu(causal_dwconv(qkv_a, conv_qkv_w[l]))
        q_a, k_a, v_a = jnp.split(qkv_a, [hA * GDN_DK, 2 * hA * GDN_DK], axis=-1)
        q_a = q_a.reshape(b, s, hA, GDN_DK)
        k_a = k_a.reshape(b, s, hA, GDN_DK)
        v_a = v_a.reshape(b, s, hA, GDN_DV)
        g_log = -jnp.exp(gdn_a_log[l].astype(jnp.float32)) * jax.nn.softplus(
            a_a.astype(jnp.float32) + gdn_dt_bias[l].astype(jnp.float32))
        beta = jax.nn.sigmoid(b_a.astype(jnp.float32))
        o_a = gdn_chunked(q_a, k_a, v_a, g_log, beta).astype(x.dtype)
        o_a = rmsnorm(o_a, gdn_norm_g[l]) * jax.nn.silu(gate_a.reshape(b, s, hA, GDN_DV))
        y_a = jnp.einsum("bse,ed->bsd", o_a.reshape(b, s, hA * GDN_DV), w_o_gdn[l])

        cq = rmsnorm(c_q, mla_q_norm_g[l])
        q_b = jnp.einsum("bsr,re->bse", cq, w_uq[l]).reshape(b, s, hB, MLA_NOPE + MLA_ROPE)
        q_nope, q_pe = q_b[..., :MLA_NOPE], rope(q_b[..., MLA_NOPE:], pos)
        ckv = rmsnorm(c_kv, mla_kv_norm_g[l])
        kv = jnp.einsum("bsr,re->bse", ckv, w_ukv[l]).reshape(b, s, hB, MLA_NOPE + MLA_V)
        k_nope, v_b = kv[..., :MLA_NOPE], kv[..., MLA_NOPE:]
        k_pe_r = rope(k_pe[:, :, None, :], pos)[:, :, 0, :]
        o_b = mla_causal(q_nope, q_pe, k_nope, k_pe_r, v_b)
        y_b = jnp.einsum("bse,ed->bsd", o_b.reshape(b, s, hB * MLA_V), w_o_mla[l])

        merged = jax.nn.sigmoid(gate_br_a) * y_a + jax.nn.sigmoid(gate_br_b) * y_b
        x = x + jnp.einsum("bsd,de->bse", merged, w_out[l])

        h = rmsnorm(x, norm_ffn_g[l])
        u = causal_dwconv(jnp.einsum("bsd,df->bsf", h, w_up[l]), conv_ffn_w[l])
        gate_f, up_f = u[..., :D_FF], u[..., D_FF:]
        x = x + jnp.einsum("bsf,fd->bsd", jax.nn.silu(gate_f) * up_f, w_down[l])
    return rmsnorm(x, norm_final_g)


SSD_EXPAND = 2
SSD_D_INNER = SSD_EXPAND * D_MODEL
SSD_HEAD_DIM = 64
SSD_N_HEADS = SSD_D_INNER // SSD_HEAD_DIM
SSD_N_GROUPS = 4
SSD_D_STATE = 128
SSD_CONV = 4
SSD_CHUNK = 128
SSD_CONV_DIM = SSD_D_INNER + 2 * SSD_N_GROUPS * SSD_D_STATE
ATT_HEAD_DIM = 64
ATT_N_HEADS = D_MODEL // ATT_HEAD_DIM
ATT_N_KV = 4
ATT_WINDOW = 128
ATT_BLOCK = 128
ATT_SCALE = ATT_HEAD_DIM ** -0.5
ROPE_THETA_2 = 500000.0
ROPE_DIM = ATT_HEAD_DIM // 4
MOE_N_GROUPS = 8
MOE_EXPERTS_PER_GROUP = 8
MOE_N_EXPERTS = MOE_N_GROUPS * MOE_EXPERTS_PER_GROUP
MOE_TOP_K = 2
MOE_D_FF = 256
MOE_BLOCK = 128
RMS_EPS = 1e-6

COL_Z = SSD_D_INNER
COL_XBC = SSD_CONV_DIM
COL_DT = SSD_N_HEADS
COL_Q = ATT_N_HEADS * ATT_HEAD_DIM
COL_K = ATT_N_KV * ATT_HEAD_DIM
COL_V = ATT_N_KV * ATT_HEAD_DIM
COL_GATE = D_MODEL
IN_COLS = COL_Z + COL_XBC + COL_DT + COL_Q + COL_K + COL_V + 2 * COL_GATE
IN_SPLITS = (COL_Z,
             COL_Z + COL_XBC,
             COL_Z + COL_XBC + COL_DT,
             COL_Z + COL_XBC + COL_DT + COL_Q,
             COL_Z + COL_XBC + COL_DT + COL_Q + COL_K,
             COL_Z + COL_XBC + COL_DT + COL_Q + COL_K + COL_V,
             COL_Z + COL_XBC + COL_DT + COL_Q + COL_K + COL_V + COL_GATE)


def rms_norm(t, g):
    tf = t.astype(jnp.float32)
    tf = tf * lax.rsqrt(jnp.mean(tf * tf, axis=-1, keepdims=True) + RMS_EPS)
    return (tf * g.astype(jnp.float32)).astype(t.dtype)

def ssd_branch(z, xbc, dt_raw, conv_w, conv_b, dt_bias, a_log, d_skip, ssd_norm_g):
    b, s, _ = xbc.shape
    G, J, P, N, L = SSD_N_GROUPS, SSD_N_HEADS // SSD_N_GROUPS, SSD_HEAD_DIM, SSD_D_STATE, SSD_CHUNK
    nc = s // L
    xbc = lax.conv_general_dilated(xbc, conv_w[:, None, :].astype(xbc.dtype), window_strides=(1,),
                                   padding=[(SSD_CONV - 1, 0)], dimension_numbers=('NWC', 'WIO', 'NWC'),
                                   feature_group_count=SSD_CONV_DIM) + conv_b
    xbc = jax.nn.silu(xbc)
    xs, bm, cm = jnp.split(xbc, [SSD_D_INNER, SSD_D_INNER + G * N], axis=-1)
    xs = xs.reshape(b, nc, L, G, J, P)
    bm = bm.reshape(b, nc, L, G, N)
    cm = cm.reshape(b, nc, L, G, N)
    dt = jax.nn.softplus(dt_raw.astype(jnp.float32) + dt_bias.astype(jnp.float32))
    a = -jnp.exp(a_log.astype(jnp.float32))
    dt_c = dt.reshape(b, nc, L, G, J)
    a_cum = jnp.cumsum(dt_c * a.reshape(G, J), axis=2)
    xdt = xs * dt_c[..., None].astype(xs.dtype)
    causal = (jnp.arange(L)[:, None] >= jnp.arange(L)[None, :])[None, None, :, :, None, None]
    seg = a_cum[:, :, :, None] - a_cum[:, :, None, :]
    decay = jnp.exp(jnp.where(causal, seg, -jnp.inf)).astype(xs.dtype)
    cb = jnp.einsum('bclgn,bcsgn->bclsg', cm, bm)
    y_diag = jnp.einsum('bclsgj,bcsgjp->bclgjp', cb[..., None] * decay, xdt)
    decay_to_end = jnp.exp(a_cum[:, :, -1:] - a_cum).astype(xs.dtype)
    states = jnp.einsum('bclgn,bclgjp->bcgjpn', bm, xdt * decay_to_end[..., None])
    chunk_decay = jnp.exp(a_cum[:, :, -1]).astype(states.dtype)

    def step(carry, inp):
        st, dec = inp
        return carry * dec[..., None, None] + st, carry

    init = jnp.zeros((b, G, J, P, N), states.dtype)
    _, prev = lax.scan(step, init, (jnp.moveaxis(states, 1, 0), jnp.moveaxis(chunk_decay, 1, 0)))
    prev = jnp.moveaxis(prev, 0, 1)
    y_off = jnp.einsum('bclgn,bcgjpn->bclgjp', cm, prev) * jnp.exp(a_cum)[..., None].astype(xs.dtype)
    y = (y_diag + y_off + xs * d_skip.reshape(G, J)[:, :, None].astype(xs.dtype)).reshape(b, s, SSD_D_INNER)
    yz = (y * jax.nn.silu(z)).reshape(b, s, G, SSD_D_INNER // G)
    return rms_norm(yz, ssd_norm_g.reshape(G, -1)).reshape(b, s, SSD_D_INNER)

def partial_rope(t, cos, sin):
    half = ROPE_DIM // 2
    t1, t2, rest = t[..., :half], t[..., half:ROPE_DIM], t[..., ROPE_DIM:]
    cos = cos.astype(t.dtype)
    sin = sin.astype(t.dtype)
    return jnp.concatenate([t1 * cos - t2 * sin, t2 * cos + t1 * sin, rest], axis=-1)

def swa_sink_branch(q, k, v, positions, q_norm_g, k_norm_g, sinks):
    b, s, _ = q.shape
    HD, KV, QG, BLK = ATT_HEAD_DIM, ATT_N_KV, ATT_N_HEADS // ATT_N_KV, ATT_BLOCK
    nb = s // BLK
    q = rms_norm(q.reshape(b, s, ATT_N_HEADS, HD), q_norm_g)
    k = rms_norm(k.reshape(b, s, KV, HD), k_norm_g)
    v = v.reshape(b, s, KV, HD)
    inv_freq = ROPE_THETA_2 ** (-jnp.arange(0, ROPE_DIM, 2, dtype=jnp.float32) / ROPE_DIM)
    ang = positions.astype(jnp.float32)[..., None] * inv_freq
    cos, sin = jnp.cos(ang)[:, :, None, :], jnp.sin(ang)[:, :, None, :]
    q = partial_rope(q, cos, sin)
    k = partial_rope(k, cos, sin)
    qb = q.reshape(b, nb, BLK, KV, QG, HD)
    kb = k.reshape(b, nb, BLK, KV, HD)
    vb = v.reshape(b, nb, BLK, KV, HD)
    pad = ((0, 0), (1, 0), (0, 0), (0, 0), (0, 0))
    kk = jnp.concatenate([jnp.pad(kb, pad)[:, :-1], kb], axis=2)
    vv = jnp.concatenate([jnp.pad(vb, pad)[:, :-1], vb], axis=2)
    scores = jnp.einsum('bnqhgd,bnkhd->bnhgqk', qb, kk).astype(jnp.float32) * ATT_SCALE
    qi = jnp.arange(nb)[:, None, None] * BLK + jnp.arange(BLK)[None, :, None]
    ki = (jnp.arange(nb)[:, None, None] - 1) * BLK + jnp.arange(2 * BLK)[None, None, :]
    diff = qi - ki
    mask = (diff >= 0) & (diff < ATT_WINDOW) & (ki >= 0)
    scores = jnp.where(mask[None, :, None, None], scores, -jnp.inf)
    sink = sinks.astype(jnp.float32).reshape(KV, QG)[None, None, :, :, None]
    m = jnp.maximum(jnp.max(scores, axis=-1), sink)
    p = jnp.exp(scores - m[..., None])
    denom = jnp.sum(p, axis=-1) + jnp.exp(sink - m)
    p = (p / denom[..., None]).astype(v.dtype)
    out = jnp.einsum('bnhgqk,bnkhd->bnqhgd', p, vv)
    return out.reshape(b, s, ATT_N_HEADS * HD)

def hier_moe(h2, w_rg, b_rg, w_re, b_re, w_gate_e, w_up_e, w_down_e):
    t = h2.shape[0]
    rows = jnp.arange(t)
    g_logits = jnp.dot(h2, w_rg).astype(jnp.float32) + b_rg.astype(jnp.float32)
    g_prob = jax.nn.softmax(g_logits, axis=-1)
    g_sel = jnp.argmax(g_logits, axis=-1).astype(jnp.int32)
    p_group = g_prob[rows, g_sel]
    e_logits_all = jnp.einsum('td,gde->tge', h2, w_re).astype(jnp.float32) + b_re.astype(jnp.float32)
    e_logits = e_logits_all[rows, g_sel]
    top_v, top_i = lax.top_k(e_logits, MOE_TOP_K)
    gate = p_group[:, None] * jax.nn.softmax(top_v, axis=-1)
    expert_id = g_sel[:, None] * MOE_EXPERTS_PER_GROUP + top_i.astype(jnp.int32)
    n_assign = t * MOE_TOP_K
    flat_e = expert_id.reshape(-1)
    flat_w = gate.reshape(-1)
    flat_t = jnp.arange(n_assign, dtype=jnp.int32) // MOE_TOP_K
    order = jnp.argsort(flat_e)
    sorted_e = flat_e[order]
    counts = jnp.bincount(flat_e, length=MOE_N_EXPERTS)
    starts = jnp.cumsum(counts) - counts
    padded = (counts + MOE_BLOCK - 1) // MOE_BLOCK * MOE_BLOCK
    padded_end = jnp.cumsum(padded)
    padded_start = padded_end - padded
    dest = padded_start[sorted_e] + jnp.arange(n_assign) - starts[sorted_e]
    n_rows = n_assign + MOE_N_EXPERTS * MOE_BLOCK
    n_blocks = n_rows // MOE_BLOCK
    tok = jnp.zeros((n_rows,), jnp.int32).at[dest].set(flat_t[order])
    wt = jnp.zeros((n_rows,), jnp.float32).at[dest].set(flat_w[order])
    block_e = jnp.minimum(jnp.searchsorted(padded_end, jnp.arange(n_blocks) * MOE_BLOCK, side='right'),
                          MOE_N_EXPERTS - 1)
    xs = h2[tok].reshape(n_blocks, MOE_BLOCK, -1)

    def expert_block(args):
        xb, e = args
        hid = jax.nn.silu(xb @ w_gate_e[e]) * (xb @ w_up_e[e])
        return hid @ w_down_e[e]

    ys = lax.map(expert_block, (xs, block_e)).reshape(n_rows, -1)
    return jnp.zeros_like(h2).at[tok].add(ys * wt[:, None].astype(ys.dtype))

def hybrid_layer(x, positions, norm1_g, w_in, conv_w, conv_b, dt_bias, a_log, d_skip, ssd_norm_g,
                 w_ssd_out, q_norm_g, k_norm_g, sinks, w_attn_out, w_out, norm2_g, w_router_group,
                 b_router_group, w_router_expert, b_router_expert, w_gate_e, w_up_e, w_down_e):
    b, s, d = x.shape
    h = rms_norm(x, norm1_g)
    proj = h @ w_in
    z, xbc, dt_raw, q, k, v, g_ssd, g_att = jnp.split(proj, IN_SPLITS, axis=-1)
    y_ssd = ssd_branch(z, xbc, dt_raw, conv_w, conv_b, dt_bias, a_log, d_skip, ssd_norm_g) @ w_ssd_out
    y_att = swa_sink_branch(q, k, v, positions, q_norm_g, k_norm_g, sinks) @ w_attn_out
    merged = jax.nn.sigmoid(g_ssd) * y_ssd + jax.nn.sigmoid(g_att) * y_att
    x = x + merged @ w_out
    h2 = rms_norm(x, norm2_g).reshape(b * s, d)
    y_moe = hier_moe(h2, w_router_group, b_router_group, w_router_expert, b_router_expert,
                     w_gate_e, w_up_e, w_down_e)
    return x + y_moe.reshape(b, s, d)

def second_inputs(seed: int = 0) -> dict:
    key = jax.random.key(seed)
    ks = jax.random.split(key, 24)
    L = DEPTH

    def nrm(k, shape, scale):
        return jax.random.normal(k, shape, jnp.float32) * scale

    x = nrm(ks[0], (BATCH, SEQ, D_MODEL), 1.0)
    positions = (jax.random.randint(ks[1], (BATCH, 1), 0, 1024, dtype=jnp.int32)
                 + jnp.arange(SEQ, dtype=jnp.int32)[None, :])
    dt0 = jnp.exp(jax.random.uniform(ks[6], (L, SSD_N_HEADS), jnp.float32,
                                     minval=math.log(1e-3), maxval=math.log(1e-1)))
    return {
        'x': x,
        'positions': positions,
        'norm1_g': 1.0 + nrm(ks[2], (L, D_MODEL), 0.02),
        'w_in': nrm(ks[3], (L, D_MODEL, IN_COLS), D_MODEL ** -0.5),
        'conv_w': nrm(ks[4], (L, SSD_CONV, SSD_CONV_DIM), SSD_CONV ** -0.5),
        'conv_b': nrm(ks[5], (L, SSD_CONV_DIM), 0.02),
        'dt_bias': dt0 + jnp.log(-jnp.expm1(-dt0)),
        'a_log': jnp.log(jax.random.uniform(ks[7], (L, SSD_N_HEADS), jnp.float32, minval=1.0, maxval=16.0)),
        'd_skip': 1.0 + nrm(ks[8], (L, SSD_N_HEADS), 0.1),
        'ssd_norm_g': 1.0 + nrm(ks[9], (L, SSD_D_INNER), 0.02),
        'w_ssd_out': nrm(ks[10], (L, SSD_D_INNER, D_MODEL), SSD_D_INNER ** -0.5),
        'q_norm_g': 1.0 + nrm(ks[11], (L, ATT_HEAD_DIM), 0.02),
        'k_norm_g': 1.0 + nrm(ks[12], (L, ATT_HEAD_DIM), 0.02),
        'sinks': nrm(ks[13], (L, ATT_N_HEADS), 0.5),
        'w_attn_out': nrm(ks[14], (L, ATT_N_HEADS * ATT_HEAD_DIM, D_MODEL), (ATT_N_HEADS * ATT_HEAD_DIM) ** -0.5),
        'w_out': nrm(ks[15], (L, D_MODEL, D_MODEL), D_MODEL ** -0.5),
        'norm2_g': 1.0 + nrm(ks[16], (L, D_MODEL), 0.02),
        'w_router_group': nrm(ks[17], (L, D_MODEL, MOE_N_GROUPS), D_MODEL ** -0.5),
        'b_router_group': nrm(ks[18], (L, MOE_N_GROUPS), 0.01),
        'w_router_expert': nrm(ks[19], (L, MOE_N_GROUPS, D_MODEL, MOE_EXPERTS_PER_GROUP), D_MODEL ** -0.5),
        'b_router_expert': nrm(ks[20], (L, MOE_N_GROUPS, MOE_EXPERTS_PER_GROUP), 0.01),
        'w_gate_e': nrm(ks[21], (L, MOE_N_EXPERTS, D_MODEL, MOE_D_FF), D_MODEL ** -0.5),
        'w_up_e': nrm(ks[22], (L, MOE_N_EXPERTS, D_MODEL, MOE_D_FF), D_MODEL ** -0.5),
        'w_down_e': nrm(ks[23], (L, MOE_N_EXPERTS, MOE_D_FF, D_MODEL), MOE_D_FF ** -0.5),
    }

def second_block(x, positions, norm1_g, w_in, conv_w, conv_b, dt_bias, a_log, d_skip, ssd_norm_g,
              w_ssd_out, q_norm_g, k_norm_g, sinks, w_attn_out, w_out, norm2_g, w_router_group,
              b_router_group, w_router_expert, b_router_expert, w_gate_e, w_up_e, w_down_e):
    for l in range(DEPTH):
        x = hybrid_layer(x, positions, norm1_g[l], w_in[l], conv_w[l], conv_b[l], dt_bias[l], a_log[l],
                         d_skip[l], ssd_norm_g[l], w_ssd_out[l], q_norm_g[l], k_norm_g[l], sinks[l],
                         w_attn_out[l], w_out[l], norm2_g[l], w_router_group[l], b_router_group[l],
                         w_router_expert[l], b_router_expert[l], w_gate_e[l], w_up_e[l], w_down_e[l])
    return x


def setup_inputs(seed=0):
    out = dict(first_inputs(seed))
    for name, value in second_inputs(seed + 1).items():
        if name != "x":
            out[name + "_2"] = value
    return out


def reference(
    x, norm_mix_g, w_in, conv_qkv_w, gdn_a_log, gdn_dt_bias, gdn_norm_g, mla_q_norm_g, w_uq,
    mla_kv_norm_g, w_ukv, w_o_gdn, w_o_mla, w_out, norm_ffn_g, w_up, conv_ffn_w, w_down,
    norm_final_g, positions_2, norm1_g_2, w_in_2, conv_w_2, conv_b_2, dt_bias_2, a_log_2,
    d_skip_2, ssd_norm_g_2, w_ssd_out_2, q_norm_g_2, k_norm_g_2, sinks_2, w_attn_out_2, w_out_2,
    norm2_g_2, w_router_group_2, b_router_group_2, w_router_expert_2, b_router_expert_2,
    w_gate_e_2, w_up_e_2, w_down_e_2,
):
    x = first_block(
        x, norm_mix_g, w_in, conv_qkv_w, gdn_a_log, gdn_dt_bias, gdn_norm_g, mla_q_norm_g, w_uq,
        mla_kv_norm_g, w_ukv, w_o_gdn, w_o_mla, w_out, norm_ffn_g, w_up, conv_ffn_w, w_down,
        norm_final_g,
    )
    return second_block(
        x, positions_2, norm1_g_2, w_in_2, conv_w_2, conv_b_2, dt_bias_2, a_log_2, d_skip_2,
        ssd_norm_g_2, w_ssd_out_2, q_norm_g_2, k_norm_g_2, sinks_2, w_attn_out_2, w_out_2,
        norm2_g_2, w_router_group_2, b_router_group_2, w_router_expert_2, b_router_expert_2,
        w_gate_e_2, w_up_e_2, w_down_e_2,
    )


_drawn_inputs = setup_inputs


def setup_inputs(seed=0):
    import zlib

    import numpy as np

    out = dict(_drawn_inputs(seed))
    spreads = {}
    factors = {'mla_q_norm_g': 5.277,
     'mla_kv_norm_g': 2.962,
     'conv_b_2': 3.19,
     'ssd_norm_g_2': 3.843,
     'q_norm_g_2': 7.802,
     'k_norm_g_2': 8.0,
     'sinks_2': 52.976,
     'norm2_g_2': 2.867,
     'b_router_group_2': 7.979,
     'b_router_expert_2': 5.308}
    for name, (base, spread) in spreads.items():
        noise = np.random.default_rng([zlib.crc32(name.encode()), seed]).standard_normal(out[name].shape)
        drawn = base * np.exp(spread * noise) if base else spread * noise
        out[name] = __import__('jax').numpy.asarray(drawn.astype(out[name].dtype))
    for name, factor in factors.items():
        out[name] = (out[name] * factor).astype(out[name].dtype)
    return out
```

```python
from contextlib import ExitStack

import numpy as np
import concourse.bass as bass
from concourse import mybir

F32 = mybir.dt.float32
I32 = mybir.dt.int32
U32 = mybir.dt.uint32
ALU = mybir.AluOpType
ACT = mybir.ActivationFunctionType
AX = mybir.AxisListType

P = 128
SEQ = 256
TT = SEQ // P
D = 1024
KD = D // P
EPS = 1e-6
NEG = -1e30
HEADS = 8
PROB = TT * HEADS
LEVELS = 7
Q_RANK, KV_RANK = 384, 256
KQ, KKV = Q_RANK // P, KV_RANK // P
ROPE = 64
D_FF = 2816
KF = D_FF // P
MLA_SCALE = float(128 + ROPE) ** -0.5
SSD_GROUPS, SSD_HEADS = 4, 32
GH = SSD_HEADS // SSD_GROUPS
D_IN2 = 2048
A_HEADS, A_KV, A_DIM = 16, 4, 64
QK_HEADS = A_HEADS + A_KV
ATT_SCALE = float(A_DIM) ** -0.5
ROPE2 = 16
EXPERTS, EGROUPS, EPG = 64, 8, 8
E_FF = 256
CAP = 32
GROUP = P // CAP
OVER = 2 * SEQ // CAP
OWN_GROUPS = EXPERTS // GROUP
GROUPS = (EXPERTS + OVER) // GROUP
RING = 6
SLOT = 2048

COLS = dict(norm_mix=8, conv_qkv=96, gdn_norm=1, mla_q=3, mla_kv=2, norm_ffn=8, conv_ffn=132,
            norm_final=8, norm1=8, conv2=96, conv_b=24, ssd_norm=16, norm2=8)
ROWS = dict(a_log=8, dt_bias=8, dt_bias2=32, a_log2=32, d_skip=32, q_gain=64, k_gain=64, sinks=16,
            b_router=72)
CONSTS = dict(ident=128, upto=128, before=128, ones=128, neg_late=128, level=LEVELS * 128, rope_cos=256,
              rope_sin=256, swap=128, mla_mask=384, swa_mask=384, iota=128, part=2, inv_freq=8, eps=1)


def offsets(sizes):
    at, out = 0, {}
    for name, n in sizes.items():
        out[name] = (at, n)
        at += n
    return out, at


COL_AT, NCOL = offsets(COLS)
ROW_AT, NROW = offsets(ROWS)
CON_AT, NCON = offsets(CONSTS)

UNITS = ([("w_lat", i, 2048) for i in range(3)] + [("w_qkv", i, 2048) for i in range(12)]
         + [("w_gates", i, 2048) for i in range(12)]
         + [("w_uq", i, 1536) for i in range(3)] + [("w_ukv", i, 2048) for i in range(2)]
         + [("w_o_gdn", i, 2048) for i in range(4)] + [("w_o_mla", i, 2048) for i in range(4)]
         + [("w_out", i, 2048) for i in range(4)]
         + [("w_up", i, 2048) for i in range(22)] + [("w_down", i, 1408) for i in range(16)]
         + [("w_xbc2", i, 2048) for i in range(12)] + [("w_z2", i, 2048) for i in range(8)]
         + [("w_att2", i, 2048) for i in range(6)] + [("w_gates2", i, 2048) for i in range(8)]
         + [("w_ssd_out2", i, 2048) for i in range(8)] + [("w_attn_out2", i, 2048) for i in range(4)]
         + [("w_out2", i, 2048) for i in range(4)])
ROUND = ([("gate", 0), ("up", 0)] + [("scatter_last", k) for k in range(4)] + [("gate", 1), ("up", 1), ("turn", 0)]
         + [("gather_next", k) for k in range(4)] + [("turn", 1), ("down", 0), ("down", 1)])
NPR = len(ROUND)
assert NPR % 8 == 0
EXPERT_UNITS = [(name, j) for name in ("w_gate_e", "w_up_e", "w_down_e") for j in range(GROUP)]
EXPERT_READER = {"w_gate_e": ("gate", 1), "w_up_e": ("up", 1), "w_down_e": ("down", 1)}


def build(nc, A, out):
    ctx = ExitStack()
    with ctx:
        sems = {}

        def S(name):
            if name not in sems:
                sems[name] = ctx.enter_context(nc.semaphore(name))
            return sems[name]

        def sb(name, shape, dt=F32):
            return ctx.enter_context(nc.sbuf_tensor(name, shape, dt))

        bank = [ctx.enter_context(nc.psum_tensor(f"bank{b}", [P, 512], F32)) for b in range(8)]
        ring = [sb(f"ring{s}", [P, SLOT]) for s in range(RING)]
        col_sb, row_sb, con_sb = sb("col_sb", [P, NCOL]), sb("row_sb", [P, NROW]), sb("con_sb", [P, NCON])
        w_ab, w_dt, w_rt = sb("w_ab", [P, KD, 16]), sb("w_dt", [P, KD, 32]), sb("w_rt", [P, KD, 72])
        pos_sb = sb("pos_sb", [P, TT], I32)
        xT, hT = sb("xT", [P, KD, SEQ]), sb("hT", [P, KD, SEQ])

        def col(name, i=0, n=1):
            at = COL_AT[name][0] + i
            return col_sb[:, at:at + n]

        def row(name):
            at, n = ROW_AT[name]
            return row_sb[:, at:at + n]

        def con(name):
            at, n = CON_AT[name]
            return con_sb[:, at:at + n]

        ident, upto, before, ones = con("ident"), con("upto"), con("before"), con("ones")
        levels = con("level").rearrange("p (s i) -> p s i", s=LEVELS)
        eps = con("eps")

        WORK = 25088
        work = sb("work", [P, WORK])

        def area(at, *shape):
            n = int(np.prod(shape))
            assert at + n <= WORK
            v = work[:, at:at + n]
            if len(shape) == 2:
                v = v.rearrange("p (a b) -> p a b", a=shape[0])
            if len(shape) == 3:
                v = v.rearrange("p (a b c) -> p a b c", a=shape[0], b=shape[1])
            return v

        sq = sb("sq", [P, 2048])
        qkvT = area(0, 24, SEQ)
        ffT = area(0, KF, SEQ)
        mergedT = area(2048, KD, SEQ)
        oaT = area(0, KD, SEQ)
        vb = area(4096, PROB, P)
        gateT, gA, gB = area(6144, KD, SEQ), area(8192, KD, SEQ), area(10240, KD, SEQ)
        latT = area(12288, 6, SEQ)
        LT, T, TTr, AT = (area(13824 + 2048 * i, PROB, P) for i in range(4))
        decay1 = area(15872, 4, 512)
        BT = area(22016, 2, 512)
        Y = area(23040, 2, 512)
        St = area(23040, HEADS, P)
        eg = sq[:, 0:1024].rearrange("p (h i) -> p h i", h=HEADS)
        kd = sq[:, 1024:2048].rearrange("p (h i) -> p h i", h=HEADS)
        qnT, knT, v_tok = area(13824, KD, SEQ), area(15872, KD, SEQ), area(17920, TT, D)
        obT = qnT
        sc1, PT1 = area(19968, 2, 384), area(20736, 2, 384)
        qpeT = area(22016, 4, SEQ)
        xbcT = area(0, 24, SEQ)
        ysT = area(0, 16, SEQ)
        state = area(6144, SSD_GROUPS, 512)
        zs = area(8192, TT, D_IN2)
        qkv_tok = area(12288, TT, 1536)
        xs_tok = area(15360, TT, D_IN2)
        xdt = area(19456, 2, 512)
        bm_tok = area(20480, SSD_GROUPS, P)
        CB = area(20992, TT, 512)
        xde = area(22016, 2, 512)
        decay2 = area(23040, 4, 512)
        qT2, kT2 = area(15360, KD, SEQ), area(17408, A_KV, SEQ)
        kdup = area(18432, TT, A_KV, P)
        qk_sq = area(19456, TT, QK_HEADS * A_DIM)
        sc2, PT2 = area(19456, 2, 384), area(20224, 2, 384)
        rope_t = area(22016, 4, TT * QK_HEADS * 8)
        oswT = area(4096, KD, SEQ)
        merged2T = area(6144, KD, SEQ)
        h2_tok = area(0, TT, D)
        xg = area(2048, KD, P)
        hid = area(3072, 2, P)
        hid_t = area(3328, 2, P)
        hidT = area(3584, 2, P)
        y_slot = area(4608, D)
        sel = area(5632, TT, P)
        sel_t = area(5888, TT, P)
        selw = area(6144, SEQ)
        selw_t = area(6400, SEQ)
        d_row = area(6656, 2, SEQ)
        g_row = area(7168, 2, SEQ)
        rt = area(7680, TT, 512)
        rtx = area(8704, 640)
        own_to_over = area(9344, EXPERTS)
        wide = area(12288, 6, SLOT)

        cv = sb("cv", [P, 2, 512])
        rs = sb("rs", [P, 2, 512])
        tmp = sb("tmp", [P, 2, 512])
        stat = sb("stat", [P, 16, 12])
        sm = sb("sm", [P, 512])

        def small(at, n):
            return sm[:, at:at + n]

        ab, glog, beta, gcum = small(0, 32), small(32, 16), small(48, 16), small(64, 16)
        sp_t, sp_e, ngc, beg, kds, expA = (small(80, 16), small(96, 16), small(112, 16), small(128, 16),
                                           small(144, 8), small(152, 8))
        dt_, dt_t, dt_e, dA, nac, eac, expA2 = (small(160, 64), small(224, 64), small(288, 64), small(352, 64),
                                                small(0, 64), small(64, 64), small(416, 32))
        de, ssq = small(448, 32), small(480, 8)
        sm2 = sb("sm2", [P, 320])
        sin2, cos2, ang = sm2[:, 0:16], sm2[:, 16:32], sm2[:, 32:48]
        rnd, red, pos_f = sm2[:, 48:80], sm2[:, 80:112], sm2[:, 112:114]
        qk_ss = sm2[:, 120:160]
        qk_r = sm2[:, 160:200]
        ridx = sb("ridx", [P, TT, 16], U32)
        be_row = sb("be_row", [1, 2 * P], I32)

        block = ctx.enter_context(nc.Block())
        product = {}
        unit_product = []
        free_sem = [S(f"bank_free{b}") for b in range(8)]
        landed = [S(f"weights_landed{s}") for s in range(RING)]
        product_ready = S("product_ready")

        def number(*key):
            return product[key if len(key) > 1 else key[0]]

        def at(*key):
            return bank[number(*key) % 8]

        def made(*key):
            return number(*key) + 1

        def bank_free(*key):
            return free_sem[number(*key) % 8]

        def used(*key):
            return number(*key) // 8 + 1

        def counter():
            seen = {}

            def nth(name, more=1):
                seen[name] = seen.get(name, 0) + more
                return seen[name]
            return nth

        def round_bank(*name):
            return ROUND.index(name) % 8

        def round_made(i, *name):
            return i * NPR + (product["base"] + ROUND.index(name) + 1)

        def round_used(i, *name):
            return i * (NPR // 8) + (product["base"] // 8 + ROUND.index(name) // 8 + 1)

        def expert_slot(n):
            return wide[:, n, :] if n < 6 else ring[(len(UNITS) + n) % RING][:, :]

        expert_landed = [S(f"expert_weights_landed{n}") for n in range(3 * GROUP)]

        def b3(ap, n, inner):
            return ap[:, :, None].to_broadcast([P, n, inner])

        def rep(ap, n, inner):
            return ap[:, None, :].to_broadcast([P, n, inner])

        def quads(ap, n=4):
            return ap.rearrange("p (a b) -> p a b", a=n)

        @block.tensor
        def _(pe):
            nth = counter()
            mm = nc.tensor.matmul

            def new(*key):
                product[key if len(key) > 1 else key[0]] = len(product)
                return bank[(len(product) - 1) % 8]



            def take_unit(name):
                u = len(unit_product)
                assert UNITS[u][0] == name
                unit_product.append(None)
                pe.wait_ge(landed[u % RING], 16 * (u // RING + 1))
                return ring[u % RING]

            def unit_read():
                unit_product[-1] = len(product) - 1

            def norm_sum(key, kt=KD, src=sq):
                pe.wait_ge(S("squares"), nth("squares"))
                b = new(key)
                if used(key) > 1:
                    pe.wait_ge(bank_free(key), used(key) - 1)
                for k in range(kt):
                    m = mm(b[:, 0:SEQ], ones, src[:, k * SEQ:(k + 1) * SEQ], start=(k == 0), stop=(k == kt - 1))
                m.then_inc(product_ready, 1)

            def to_features(key, name, src, kt=KD):
                w = take_unit(name)[:, 0:kt * 256].rearrange("p (k n) -> p k n", k=kt)
                b = new(key)
                if used(key) > 1:
                    pe.wait_ge(bank_free(key), used(key) - 1)
                for j in range(2):
                    for k in range(kt):
                        m = mm(b[:, j * SEQ:(j + 1) * SEQ], w[:, k, j * P:(j + 1) * P], src[:, k, :],
                               start=(k == 0), stop=(k == kt - 1))
                m.then_inc(product_ready, 1)
                unit_read()

            def to_tokens(key, name, src):
                w = take_unit(name).rearrange("p (k n) -> p k n", k=KD)
                b = new(key)
                pe.wait_ge(bank_free(key), used(key) - 1)
                for t in range(TT):
                    for k in range(KD):
                        m = mm(b[:, t * 256:(t + 1) * 256], src[:, k, t * P:(t + 1) * P], w[:, k, :],
                               start=(k == 0), stop=(k == KD - 1))
                m.then_inc(product_ready, 1)
                unit_read()

            def small_tokens(key, w, n, src):
                b = new(key)
                if used(key) > 1:
                    pe.wait_ge(bank_free(key), used(key) - 1)
                for t in range(TT):
                    for k in range(KD):
                        m = mm(b[:, t * n:(t + 1) * n], src[:, k, t * P:(t + 1) * P], w[:, k, :],
                               start=(k == 0), stop=(k == KD - 1))
                m.then_inc(product_ready, 1)

            def split_features(key, name, src, kt, units_per_tile, tiles=2):
                b = new(key)
                pe.wait_ge(bank_free(key), used(key) - 1)
                first = len(unit_product)
                total = kt * units_per_tile
                for j in range(tiles):
                    for h in range(units_per_tile):
                        w = take_unit(name)[:, 0:kt * P].rearrange("p (k n) -> p k n", k=kt)
                        for k in range(kt):
                            kk = h * kt + k
                            m = mm(b[:, j * SEQ:(j + 1) * SEQ], w[:, k, :], src[:, kk, :],
                                   start=(kk == 0), stop=(kk == total - 1))
                m.then_inc(product_ready, 1)
                for u in range(first, len(unit_product)):
                    unit_product[u] = len(product) - 1

            pe.wait_ge(S("loads"), nth("loads", 16 * 4))
            norm_sum("norm_mix")
            pe.wait_ge(S("normed"), nth("normed"))
            small_tokens("ab", w_ab, 16, hT)
            for i in range(3):
                to_features(("lat", i), "w_lat", hT)
            for i in range(12):
                to_features(("qkv", i), "w_qkv", hT)

            pe.wait_ge(S("glog"), nth("glog"))
            b = new("gcum")
            pe.wait_ge(bank_free("gcum"), used("gcum") - 1)
            mm(b[:, 0:PROB], upto, glog, start=True, stop=True).then_inc(product_ready, 1)
            for i in range(8):
                pe.wait_ge(S("l2_squares"), nth("l2_squares"))
                b = new("l2", i)
                pe.wait_ge(bank_free("l2", i), used("l2", i) - 1)
                mm(b[:, :], ones, sq[:, (i % 2) * 512:(i % 2 + 1) * 512], start=True, stop=True).then_inc(product_ready, 1)
            for c in range(TT):
                for hq in range(2):
                    b = new("vt", c * 2 + hq)
                    pe.wait_ge(bank_free("vt", c * 2 + hq), used("vt", c * 2 + hq) - 1)
                    for p in range(4):
                        m = nc.tensor.transpose(b[:, p * P:(p + 1) * P], qkvT[:, 16 + hq * 4 + p, c * P:(c + 1) * P],
                                                ident)
                    m.then_inc(product_ready, 1)
            gates = iter(range(12))

            def fill_gate():
                i = next(gates, None)
                if i is not None:
                    to_features(("gates", i), "w_gates", hT)

            pe.wait_ge(S("l2_normed"), nth("l2_normed", 8))
            for hq in range(2):
                b = new("kt", hq)
                pe.wait_ge(bank_free("kt", hq), used("kt", hq) - 1)
                for p in range(4):
                    m = nc.tensor.transpose(b[:, p * P:(p + 1) * P], qkvT[:, 8 + hq * 4 + p, 0:P], ident)
                m.then_inc(product_ready, 1)
            for q in range(4):
                c, h0 = q // 2, (q % 2) * 4
                cs = slice(c * P, (c + 1) * P)
                for key in ("grow", "brow", "gram", "qk"):
                    b = new(key, q)
                    pe.wait_ge(bank_free(key, q), used(key, q) - 1)
                    for p in range(4):
                        pr, h = q * 4 + p, h0 + p
                        o = b[:, p * P:(p + 1) * P]
                        if key == "grow":
                            m = mm(o, glog[:, pr:pr + 1].to_broadcast([P, P]), upto, start=True, stop=True)
                        elif key == "brow":
                            m = mm(o, beta[:, pr:pr + 1].to_broadcast([P, P]), ident, start=True, stop=True)
                        elif key == "gram":
                            m = mm(o, qkvT[:, 8 + h, cs], qkvT[:, 8 + h, cs], start=True, stop=True)
                        else:
                            m = mm(o, qkvT[:, 8 + h, cs], qkvT[:, h, cs], start=True, stop=True)
                    m.then_inc(product_ready, 1)
            fill_gate()
            for q in range(4):
                pe.wait_ge(S("off_diagonal"), nth("off_diagonal"))
                b = new("Y", 0, q)
                pe.wait_ge(bank_free("Y", 0, q), used("Y", 0, q) - 1)
                for p in range(4):
                    m = mm(b[:, p * P:(p + 1) * P], BT[:, q % 2, p * P:(p + 1) * P], ident, start=True, stop=True)
                m.then_inc(product_ready, 1)
            fill_gate()
            for s in range(1, LEVELS):
                def bt_t(q):
                    pe.wait_ge(S("off_diagonal"), nth("off_diagonal"))
                    if s == 1:
                        pe.wait_ge(bank_free("Y", 0, q), used("Y", 0, q))
                    else:
                        pe.wait_ge(bank_free("TY", s - 1, q), used("TY", s - 1, q))
                        pe.wait_ge(bank_free("YT", s - 1, q), used("YT", s - 1, q))
                    b = new("Y", s, q)
                    pe.wait_ge(bank_free("Y", s, q), used("Y", s, q) - 1)
                    for p in range(4):
                        m = mm(b[:, p * P:(p + 1) * P], BT[:, q % 2, p * P:(p + 1) * P], T[:, q * 4 + p, :],
                               start=True, stop=True)
                    m.then_inc(product_ready, 1)

                def t_y(q):
                    pe.wait_ge(bank_free("Y", s, q), used("Y", s, q))
                    for key in ("TY", "YT") if s < LEVELS - 1 else ("YT",):
                        b = new(key, s, q)
                        pe.wait_ge(bank_free(key, s, q), used(key, s, q) - 1)
                        for p in range(4):
                            y, tt = Y[:, q % 2, p * P:(p + 1) * P], TTr[:, q * 4 + p, :]
                            lhs, rhs = (tt, y) if key == "TY" else (y, tt)
                            m = mm(b[:, p * P:(p + 1) * P], lhs, rhs, start=True, stop=True)
                        m.then_inc(product_ready, 1)

                bt_t(0)
                bt_t(1)
                t_y(0)
                bt_t(2)
                t_y(1)
                bt_t(3)
                t_y(2)
                t_y(3)
                fill_gate()
                fill_gate()
            for q in range(4):
                pe.wait_ge(bank_free("YT", LEVELS - 1, q), used("YT", LEVELS - 1, q))
            for hq in range(2):
                pe.wait_ge(bank_free("vt", hq), used("vt", hq))
                b = new("vn", hq)
                pe.wait_ge(bank_free("vn", hq), used("vn", hq) - 1)
                for p in range(4):
                    pr = hq * 4 + p
                    m = mm(b[:, p * P:(p + 1) * P], TTr[:, pr, :], vb[:, pr, :], start=True, stop=True)
                m.then_inc(product_ready, 1)
            for hq in range(2):
                pe.wait_ge(bank_free("kt", hq), used("kt", hq))
                pe.wait_ge(bank_free("vn", hq), used("vn", hq))
                b = new("S", hq)
                pe.wait_ge(bank_free("S", hq), used("S", hq) - 1)
                for p in range(4):
                    h = hq * 4 + p
                    m = mm(b[:, p * P:(p + 1) * P], kd[:, h, :], vb[:, h, :], start=True, stop=True)
                m.then_inc(product_ready, 1)
            for hq in range(2):
                pe.wait_ge(bank_free("S", hq), used("S", hq))
                b = new("KS", hq)
                pe.wait_ge(bank_free("KS", hq), used("KS", hq) - 1)
                for p in range(4):
                    h = hq * 4 + p
                    m = mm(b[:, p * P:(p + 1) * P], qkvT[:, 8 + h, P:SEQ], St[:, h, :], start=True, stop=True)
                m.then_inc(product_ready, 1)
            for hq in range(2):
                pe.wait_ge(S("residual"), nth("residual"))
                b = new("vn", 2 + hq)
                pe.wait_ge(bank_free("vn", 2 + hq), used("vn", 2 + hq) - 1)
                for p in range(4):
                    pr = HEADS + hq * 4 + p
                    m = mm(b[:, p * P:(p + 1) * P], TTr[:, pr, :], vb[:, pr, :], start=True, stop=True)
                m.then_inc(product_ready, 1)
            pe.wait_ge(S("q_decayed"), nth("q_decayed"))
            for hp in range(4):
                if hp % 2 == 0:
                    pe.wait_ge(bank_free("vn", 2 + hp // 2), used("vn", 2 + hp // 2))
                b = new("oa", hp)
                pe.wait_ge(bank_free("oa", hp), used("oa", hp) - 1)
                for j in range(2):
                    h = hp * 2 + j
                    o = b[:, j * SEQ:(j + 1) * SEQ]
                    mm(o[:, 0:P], vb[:, h, :], AT[:, h, :], start=True, stop=True)
                    mm(o[:, P:SEQ], St[:, h, :], qkvT[:, h, P:SEQ], start=True, stop=False)
                    m = mm(o[:, P:SEQ], vb[:, HEADS + h, :], AT[:, HEADS + h, :], start=False, stop=True)
                m.then_inc(product_ready, 1)
            for hp in range(4):
                pe.wait_ge(S("oa_squares"), nth("oa_squares"))
                b = new("oan", hp)
                pe.wait_ge(bank_free("oan", hp), used("oan", hp) - 1)
                mm(b[:, :], ones, sq[:, hp * 512:(hp + 1) * 512], start=True, stop=True).then_inc(product_ready, 1)

            pe.wait_ge(S("lat_squares"), nth("lat_squares"))
            b = new("latn")
            pe.wait_ge(bank_free("latn"), used("latn") - 1)
            for k in range(KQ):
                mm(b[:, 0:SEQ], ones, sq[:, k * SEQ:(k + 1) * SEQ], start=(k == 0), stop=(k == KQ - 1))
            for k in range(KKV):
                m = mm(b[:, SEQ:2 * SEQ], ones, sq[:, (KQ + k) * SEQ:(KQ + k + 1) * SEQ],
                       start=(k == 0), stop=(k == KKV - 1))
            m.then_inc(product_ready, 1)
            b = new("krot")
            pe.wait_ge(bank_free("krot"), used("krot") - 1)
            mm(b[:, 0:SEQ], con("swap"), latT[:, 5, :], start=True, stop=True).then_inc(product_ready, 1)
            pe.wait_ge(S("lat_normed"), nth("lat_normed"))
            for u in range(3):
                w = take_unit("w_uq")[:, 0:KQ * 512].rearrange("p (k n) -> p k n", k=KQ)
                for g in range(2):
                    b = new("uq", u * 2 + g)
                    pe.wait_ge(bank_free("uq", u * 2 + g), used("uq", u * 2 + g) - 1)
                    for j in range(2):
                        for k in range(KQ):
                            m = mm(b[:, j * SEQ:(j + 1) * SEQ], w[:, k, (g * 2 + j) * P:(g * 2 + j + 1) * P],
                                   latT[:, k, :], start=(k == 0), stop=(k == KQ - 1))
                    m.then_inc(product_ready, 1)
                unit_read()
            w = take_unit("w_ukv").rearrange("p (k n) -> p k n", k=KKV)
            for g in range(4):
                b = new("uk", g)
                pe.wait_ge(bank_free("uk", g), used("uk", g) - 1)
                for j in range(2):
                    for k in range(KKV):
                        m = mm(b[:, j * SEQ:(j + 1) * SEQ], w[:, k, (g * 2 + j) * P:(g * 2 + j + 1) * P],
                               latT[:, KQ + k, :], start=(k == 0), stop=(k == KKV - 1))
                m.then_inc(product_ready, 1)
            unit_read()
            w = take_unit("w_ukv").rearrange("p (k n) -> p k n", k=KKV)
            for t in range(TT):
                for g in range(2):
                    b = new("uv", t * 2 + g)
                    pe.wait_ge(bank_free("uv", t * 2 + g), used("uv", t * 2 + g) - 1)
                    for k in range(KKV):
                        m = mm(b[:, :], latT[:, KQ + k, t * P:(t + 1) * P], w[:, k, g * 512:(g + 1) * 512],
                               start=(k == 0), stop=(k == KKV - 1))
                    m.then_inc(product_ready, 1)
            unit_read()
            for g in range(2):
                pe.wait_ge(bank_free("uq", 4 + g), used("uq", 4 + g))
                b = new("qrot", g)
                pe.wait_ge(bank_free("qrot", g), used("qrot", g) - 1)
                mm(b[:, :], con("swap"), cv[:, g, :], start=True, stop=True).then_inc(product_ready, 1)

            def attention(name, heads, parts, value, sc, PT):
                def scores(h):
                    b = new(name + "_s", h)
                    pe.wait_ge(bank_free(name + "_s", h), used(name + "_s", h) - 1)
                    for i in range(TT):
                        o = b[:, i * P:i * P + (i + 1) * P] if i else b[:, 0:P]
                        qk = parts(h, slice(i * P, (i + 1) * P), slice(0, (i + 1) * P))
                        for n, (qq, kk) in enumerate(qk):
                            m = mm(o, qq, kk, start=(n == 0), stop=(n == len(qk) - 1))
                    m.then_inc(product_ready, 1)

                scores(0)
                for h in range(heads):
                    if h + 1 < heads:
                        scores(h + 1)
                    pe.wait_ge(S(name + "_p"), nth(name + "_p"))
                    b = new(name + "_pt", h)
                    pe.wait_ge(bank_free(name + "_pt", h), used(name + "_pt", h) - 1)
                    for n in range(3):
                        m = nc.tensor.transpose(b[:, n * P:(n + 1) * P], sc[:, h % 2, n * P:(n + 1) * P], ident)
                    m.then_inc(product_ready, 1)
                    pe.wait_ge(bank_free(name + "_pt", h), used(name + "_pt", h))
                    b = new(name + "_o", h)
                    pe.wait_ge(bank_free(name + "_o", h), used(name + "_o", h) - 1)
                    v0, v1, lo = value(h, 0), value(h, 1), (h % 2) * 64
                    n = v0.shape[1]
                    o = b[:, 0:SEQ] if n == P else b[lo:lo + n, 0:SEQ]
                    mm(o[:, 0:P], v0, PT[:, h % 2, 0:P], start=True, stop=True)
                    mm(o[:, P:SEQ], v0, PT[:, h % 2, P:2 * P], start=True, stop=False)
                    m = mm(o[:, P:SEQ], v1, PT[:, h % 2, 2 * P:3 * P], start=False, stop=True)
                    m.then_inc(product_ready, 1)

            pe.wait_ge(S("mla_in"), nth("mla_in"))
            for g in range(4):
                pe.wait_ge(bank_free("uq", g), used("uq", g))
            for g in range(4):
                pe.wait_ge(bank_free("uk", g), used("uk", g))
            for g in range(4):
                pe.wait_ge(bank_free("uv", g), used("uv", g))

            def mla_parts(h, qs, ks):
                lo = (h % 2) * ROPE
                return [(qnT[:, h, qs], knT[:, h, ks]),
                        (qpeT[lo:lo + ROPE, h // 2, qs], latT[lo:lo + ROPE, 5, ks])]

            attention("mla", HEADS, mla_parts, lambda h, t: v_tok[:, t, h * P:(h + 1) * P], sc1, PT1)
            pe.wait_ge(S("oa_done"), nth("oa_done", 4))
            for i in range(4):
                to_features(("o_gdn", i), "w_o_gdn", oaT)
            for h in range(HEADS):
                pe.wait_ge(bank_free("mla_o", h), used("mla_o", h))
            for i in range(4):
                to_features(("o_mla", i), "w_o_mla", obT)
            pe.wait_ge(S("merged"), nth("merged", 4))
            for i in range(4):
                to_features(("out1", i), "w_out", mergedT)

            norm_sum("norm_ffn")
            pe.wait_ge(S("normed"), nth("normed"))
            for i in range(KF):
                to_features(("up1", i), "w_up", hT)
            pe.wait_ge(S("ff"), nth("ff", KF))
            for i in range(4):
                split_features(("down1", i), "w_down", ffT, KF // 2, 2)
            norm_sum("norm_final")
            norm_sum("norm1")
            pe.wait_ge(S("normed"), nth("normed"))

            pe.wait_ge(S("late_loads"), nth("late_loads", 48))
            small_tokens("dt", w_dt, 32, hT)
            for i in range(12):
                to_features(("xbc", i), "w_xbc2", hT)
            for i in range(8):
                to_tokens(("z", i), "w_z2", hT)
            fills = iter([("att2", i) for i in range(6)])

            def fill2():
                key = next(fills, None)
                if key is not None:
                    to_tokens(key, "w_att2", hT)

            pe.wait_ge(S("dA"), nth("dA"))
            b = new("acum")
            pe.wait_ge(bank_free("acum"), used("acum") - 1)
            mm(b[:, 0:64], upto, dA, start=True, stop=True).then_inc(product_ready, 1)
            for i in range(12):
                pe.wait_ge(bank_free("xbc", i), used("xbc", i))
            for c in range(TT):
                for j in range(4):
                    b = new("xt", c, j)
                    pe.wait_ge(bank_free("xt", c, j), used("xt", c, j) - 1)
                    for p in range(4):
                        m = nc.tensor.transpose(b[:, p * P:(p + 1) * P], xbcT[:, j * 4 + p, c * P:(c + 1) * P], ident)
                    m.then_inc(product_ready, 1)
            b = new("bmt")
            pe.wait_ge(bank_free("bmt"), used("bmt") - 1)
            for g in range(SSD_GROUPS):
                m = nc.tensor.transpose(b[:, g * P:(g + 1) * P], xbcT[:, 16 + g, 0:P], ident)
            m.then_inc(product_ready, 1)
            for c in range(TT):
                b = new("cb", c)
                pe.wait_ge(bank_free("cb", c), used("cb", c) - 1)
                for g in range(SSD_GROUPS):
                    m = mm(b[:, g * P:(g + 1) * P], xbcT[:, 16 + g, c * P:(c + 1) * P],
                           xbcT[:, 20 + g, c * P:(c + 1) * P], start=True, stop=True)
                m.then_inc(product_ready, 1)

            def decay_rows(n):
                c, g, hq = n // 8, n % 8 // 2, n % 2
                b = new("arow", n)
                pe.wait_ge(bank_free("arow", n), used("arow", n) - 1)
                for p in range(4):
                    i = c * SSD_HEADS + g * GH + hq * 4 + p
                    m = mm(b[:, p * P:(p + 1) * P], dA[:, i:i + 1].to_broadcast([P, P]), upto, start=True, stop=True)
                m.then_inc(product_ready, 1)

            def turn_y(n):
                pe.wait_ge(S("y_normed"), nth("y_normed"))
                b = new("ynt", n)
                pe.wait_ge(bank_free("ynt", n), used("ynt", n) - 1)
                for p in range(4):
                    m = nc.tensor.transpose(b[:, p * P:(p + 1) * P], cv[:, n % 2, p * P:(p + 1) * P], ident)
                m.then_inc(product_ready, 1)

            decay_rows(0)
            decay_rows(1)
            for n in range(TT * SSD_GROUPS):
                c, g = n // SSD_GROUPS, n % SSD_GROUPS
                if n + 1 < 8:
                    decay_rows(2 * n + 2)
                    decay_rows(2 * n + 3)
                fill2()
                if n >= 1:
                    turn_y(n - 1)
                pe.wait_ge(S("decay_mult"), nth("decay_mult", 2))
                b = new("y", n)
                pe.wait_ge(bank_free("y", n), used("y", n) - 1)
                for h in range(GH):
                    m = mm(b[:, h * 64:(h + 1) * 64], decay2[:, (2 * n + h // 4) % 4, (h % 4) * P:(h % 4 + 1) * P],
                           xdt[:, n % 2, h * 64:(h + 1) * 64], start=True, stop=True)
                m.then_inc(product_ready, 1)
                if c == 0:
                    pe.wait_ge(S("xde"), nth("xde"))
                    pe.wait_ge(bank_free("bmt"), used("bmt"))
                    b = new("st", g)
                    pe.wait_ge(bank_free("st", g), used("st", g) - 1)
                    mm(b[:, :], bm_tok[:, g, :], xde[:, g % 2, :], start=True, stop=True).then_inc(product_ready, 1)
                else:
                    if g == 0:
                        for k in range(SSD_GROUPS):
                            pe.wait_ge(bank_free("st", k), used("st", k))
                    b = new("yo", g)
                    pe.wait_ge(bank_free("yo", g), used("yo", g) - 1)
                    mm(b[:, :], xbcT[:, 20 + g, P:SEQ], state[:, g, :], start=True, stop=True).then_inc(product_ready, 1)
                if n < 6:
                    fill2()
            turn_y(7)
            for i in range(8):
                to_features(("gates2", i), "w_gates2", hT)

            pe.wait_ge(S("q_tok2"), nth("q_tok2"))
            for j in range(4):
                b = new("qt2", j)
                pe.wait_ge(bank_free("qt2", j), used("qt2", j) - 1)
                for p in range(4):
                    tile, t = j * 2 + p // 2, p % 2
                    m = nc.tensor.transpose(b[:, p * P:(p + 1) * P], qkv_tok[:, t, tile * P:(tile + 1) * P], ident)
                m.then_inc(product_ready, 1)
            for j in range(2):
                b = new("kt2", j)
                pe.wait_ge(bank_free("kt2", j), used("kt2", j) - 1)
                for p in range(4):
                    kv, t = j * 2 + p // 2, p % 2
                    m = nc.tensor.transpose(b[:, p * P:(p + 1) * P], kdup[:, t, kv, :], ident)
                m.then_inc(product_ready, 1)
            for j in range(4):
                pe.wait_ge(bank_free("qt2", j), used("qt2", j))
            for j in range(2):
                pe.wait_ge(bank_free("kt2", j), used("kt2", j))

            def swa_parts(h, qs, ks):
                lo = (h % 2) * A_DIM
                return [(qT2[lo:lo + A_DIM, h // 2, qs], kT2[lo:lo + A_DIM, h // 4, ks])]

            attention("swa", A_HEADS, swa_parts,
                      lambda h, t: qkv_tok[:, t, QK_HEADS * A_DIM + h // 4 * A_DIM:
                                             QK_HEADS * A_DIM + (h // 4 + 1) * A_DIM], sc2, PT2)
            for n in range(8):
                pe.wait_ge(bank_free("ynt", n), used("ynt", n))
            for i in range(4):
                split_features(("o_ssd", i), "w_ssd_out2", ysT, 16, 1)
            for h in range(A_HEADS):
                pe.wait_ge(bank_free("swa_o", h), used("swa_o", h))
            for i in range(4):
                to_features(("o_swa", i), "w_attn_out2", oswT)
            pe.wait_ge(S("merged"), nth("merged", 4))
            for i in range(4):
                to_features(("out2", i), "w_out2", merged2T)
            norm_sum("norm2")
            pe.wait_ge(S("normed"), nth("normed"))
            small_tokens("route", w_rt, 72, hT)
            for t in range(TT):
                for j in range(2):
                    b = new("h2t", t * 2 + j)
                    pe.wait_ge(bank_free("h2t", t * 2 + j), used("h2t", t * 2 + j) - 1)
                    for p in range(4):
                        m = nc.tensor.transpose(b[:, p * P:(p + 1) * P], hT[:, j * 4 + p, t * P:(t + 1) * P], ident)
                    m.then_inc(product_ready, 1)
            pe.wait_ge(S("chosen"), nth("chosen"))
            oh = rt[:, :, 192:256]
            b = new("counts")
            pe.wait_ge(bank_free("counts"), used("counts") - 1)
            mm(b[:, 0:64], ones, oh[:, 0, :], start=True, stop=False)
            mm(b[:, 0:64], ones, oh[:, 1, :], start=False, stop=True)
            mm(b[:, 64:128], before, oh[:, 0, :], start=True, stop=True)
            mm(b[:, 128:192], ones, oh[:, 0, :], start=True, stop=False)
            m = mm(b[:, 128:192], before, oh[:, 1, :], start=False, stop=True)
            m.then_inc(product_ready, 1)
            pe.wait_ge(S("places"), nth("places"))
            b = new("be")
            pe.wait_ge(bank_free("be"), used("be") - 1)
            mm(b[0:1, 0:P], rtx[:, 512:513], ident, start=True, stop=True).then_inc(product_ready, 1)
            for key, c0 in (("d_row", 384), ("g_row", 388)):
                b = new(key)
                pe.wait_ge(bank_free(key), used(key) - 1)
                for k in range(2):
                    for t in range(TT):
                        m = mm(b[:, k * SEQ + t * P:k * SEQ + (t + 1) * P],
                               rt[:, t, c0 + k:c0 + k + 1].to_broadcast([P, P]), ident, start=True, stop=True)
                m.then_inc(product_ready, 1)
            for n in range(4):
                pe.wait_ge(bank_free("h2t", n), used("h2t", n))
            pe.wait_ge(S("sel_ready"), 1)
            for k in range(4):
                b = new("gather", k)
                pe.wait_ge(bank_free("gather", k), used("gather", k) - 1)
                for j in range(2):
                    for t in range(TT):
                        m = mm(b[:, j * P:(j + 1) * P], h2_tok[:, t, (k * 2 + j) * P:(k * 2 + j + 1) * P],
                               sel[:, t, :], start=(t == 0), stop=(t == TT - 1))
                m.then_inc(product_ready, 1)
            while len(product) % 8:
                key = ("pad", len(product))
                b = new(key)
                pe.wait_ge(bank_free(key), used(key) - 1)
                mm(b[:, 0:1], ident, ones[:, 0:1], start=True, stop=True).then_inc(product_ready, 1)
            for k in range(4):
                pe.wait_ge(bank_free("gather", k), used("gather", k))
            base = len(product)
            product["base"] = base

            with pe.Fori(0, GROUPS) as i:
                for name, n in ROUND:
                    q = round_bank(name, n)
                    b = bank[q]
                    if name in ("gate", "up"):
                        if name == "gate" and n == 0:
                            for k in range(4):
                                pe.wait_ge(free_sem[round_bank("gather_next", k)],
                                           round_used(i, "gather_next", k) - NPR // 8)
                        first = GROUP * ("gate", "up").index(name)
                        if n == 0:
                            for j in range(GROUP):
                                pe.wait_ge(expert_landed[first + j], 16 * i + 16)
                        pe.wait_ge(free_sem[q], round_used(i, name, n) - 1)
                        for k in range(KD):
                            for j in range(GROUP):
                                w = expert_slot(first + j).rearrange("p (k n) -> p k n", k=KD)
                                m = mm(b[j * CAP:(j + 1) * CAP, 0:P], xg[:, k, j * CAP:(j + 1) * CAP],
                                       w[:, k, n * P:(n + 1) * P], start=(k == 0), stop=(k == KD - 1),
                                       tile_position=(0, j * CAP))
                        m.then_inc(product_ready, 1)
                    elif name == "turn":
                        pe.wait_ge(free_sem[round_bank("up", n)], round_used(i, "up", n))
                        pe.wait_ge(free_sem[q], round_used(i, name, n) - 1)
                        nc.tensor.transpose(b[:, 0:P], hid[:, n, :], ident).then_inc(product_ready, 1)
                    elif name == "scatter_last":
                        if n == 0:
                            pe.wait_ge(S("selw_ready"), i + 1)
                        if n % 2 == 0:
                            pe.wait_ge(free_sem[round_bank("down", n // 2)],
                                       round_used(i, "down", n // 2) - NPR // 8)
                        pe.wait_ge(free_sem[q], round_used(i, name, n) - 1)
                        for j in range(2):
                            d = n * 2 + j
                            m = mm(b[:, j * SEQ:(j + 1) * SEQ], y_slot[:, d * P:(d + 1) * P], selw[:, :],
                                   start=True, stop=True)
                        m.then_inc(product_ready, 1)
                    elif name == "gather_next":
                        if n == 0:
                            pe.wait_ge(S("sel_ready"), i + 2)
                        pe.wait_ge(free_sem[q], round_used(i, name, n) - 1)
                        for j in range(2):
                            for t in range(TT):
                                m = mm(b[:, j * P:(j + 1) * P], h2_tok[:, t, (n * 2 + j) * P:(n * 2 + j + 1) * P],
                                       sel[:, t, :], start=(t == 0), stop=(t == TT - 1))
                        m.then_inc(product_ready, 1)
                    else:
                        if n == 0:
                            for f in range(2):
                                pe.wait_ge(free_sem[round_bank("turn", f)], round_used(i, "turn", f))
                            for j in range(GROUP):
                                pe.wait_ge(expert_landed[2 * GROUP + j], 16 * i + 16)
                        pe.wait_ge(free_sem[q], round_used(i, name, n) - 1)
                        for f in range(2):
                            for j in range(GROUP):
                                w = expert_slot(2 * GROUP + j).rearrange("p (k n) -> p k n", k=2)
                                m = mm(b[j * CAP:(j + 1) * CAP, :], hidT[:, f, j * CAP:(j + 1) * CAP],
                                       w[:, f, n * 512:(n + 1) * 512], start=(f == 0), stop=(f == 1),
                                       tile_position=(0, j * CAP))
                        m.then_inc(product_ready, 1)
            pe.wait_ge(S("selw_ready"), GROUPS + 1)
            for n in range(4):
                if n % 2 == 0:
                    pe.wait_ge(free_sem[round_bank("down", n // 2)], base // 8 + GROUPS * (NPR // 8))
                pe.wait_ge(free_sem[n], base // 8 + GROUPS * (NPR // 8))
                for j in range(2):
                    d = n * 2 + j
                    m = mm(bank[n][:, j * SEQ:(j + 1) * SEQ], y_slot[:, d * P:(d + 1) * P], selw[:, :],
                           start=True, stop=True)
                m.then_inc(product_ready, 1)

        base = product["base"]
        U0 = len(UNITS)

        @block.sync
        def _(sp):
            sp.dma_start(xT[:, :, :], A["x"]).then_inc(S("x_landed"), 16)
            sp.dma_start(con_sb[:, :], A["consts"]).then_inc(S("loads"), 16)
            sp.dma_start(col_sb[:, :], A["cols"]).then_inc(S("loads"), 16)
            sp.dma_start(row_sb[:, :], A["rows"]).then_inc(S("loads"), 16)
            sp.dma_start(w_ab[:, :, :], A["w_ab"]).then_inc(S("loads"), 16)
            for u, (name, i, n) in enumerate(UNITS):
                if u >= RING:
                    sp.wait_ge(product_ready, unit_product[u - RING] + 1)
                sp.dma_start(ring[u % RING][:, 0:n], A[name][i]).then_inc(landed[u % RING], 16)
                if u == 2:
                    sp.dma_start(w_dt[:, :, :], A["w_dt"]).then_inc(S("late_loads"), 16)
                    sp.dma_start(w_rt[:, :, :], A["w_rt"]).then_inc(S("late_loads"), 16)
                    sp.dma_start(pos_sb[:, :], A["pos"]).then_inc(S("late_loads"), 16)
            for n, (name, j) in enumerate(EXPERT_UNITS):
                if n == 0:
                    sp.wait_ge(product_ready, made("o_swa", 0))
                if n >= 6:
                    sp.wait_ge(product_ready, unit_product[U0 - RING + n - 6] + 1)
                sp.dma_start(expert_slot(n), A[name][j]).then_inc(expert_landed[n], 16)
            with sp.Fori(1, OWN_GROUPS) as i:
                for n, (name, j) in enumerate(EXPERT_UNITS):
                    sp.wait_ge(product_ready, round_made(i, *EXPERT_READER[name]) - NPR)
                    sp.dma_start(expert_slot(n), A[name][bass.ds(GROUP * i + j, 1), :, :]
                                 .rearrange("a p n -> (a p) n")).then_inc(expert_landed[n], 16)
            sp.wait_ge(bank_free("be"), used("be"))
            with sp.Fori(0, GROUPS - OWN_GROUPS) as i:
                number_of = [sp.value_load(be_row[0:1, bass.ds(GROUP * i + j, 1)], min_val=0, max_val=EXPERTS)
                             for j in range(GROUP)]
                expert_of = [sp.value_load(be_row[0:1, bass.ds(GROUP * i + j + P, 1)], min_val=0,
                                           max_val=EXPERTS - 1) for j in range(GROUP)]
                for n, (name, j) in enumerate(EXPERT_UNITS):
                    e = expert_of[j]
                    sp.wait_ge(product_ready, round_made(i + OWN_GROUPS, *EXPERT_READER[name]) - NPR)
                    sp.dma_start(expert_slot(n), A[name][bass.ds(e, 1), :, :].rearrange("a p n -> (a p) n"),
                                 cond=(number_of[j] < EXPERTS)).then_inc(expert_landed[n], 16)
            for b in range(4):
                sp.wait_ge(free_sem[b], base // 8 + GROUPS * (NPR // 8) + 1)
            sp.dma_start(out, xT[:, :, :]).then_inc(S("stored"), 16)
            sp.wait_ge(S("stored"), 16)

        @block.scalar
        def _(act):
            nth = counter()
            A_ = nc.scalar.activation




            def squares_of_x(*keys):
                for key in keys:
                    act.wait_ge(bank_free(key), used(key))
                A_(sq[:, :], xT[:, :, :].rearrange("p k t -> p (k t)"), ACT.Square).then_inc(S("squares"), 1)

            def root(key):
                act.wait_ge(product_ready, made(key))
                A_(rs[:, 0, 0:SEQ], at(key)[:, 0:SEQ], ACT.Ln, bias=eps, scale=1.0 / D).then_inc(bank_free(key), 1)
                act.wait_ge(bank_free(key), used(key))
                A_(rs[:, 0, 0:SEQ], rs[:, 0, 0:SEQ], ACT.Exp, scale=-0.5).then_inc(S("rs_ready"), 1)

            act.wait_ge(S("x_landed"), nth("x_landed", 16))
            squares_of_x()
            act.wait_ge(S("loads"), nth("loads", 64))
            root("norm_mix")
            act.wait_ge(S("sp_in"), nth("sp_in"))
            A_(expA, row("a_log"), ACT.Exp)
            A_(ab[:, 16:32], ab[:, 16:32], ACT.Exp, scale=-1.0)
            A_(sp_e, sp_t, ACT.Exp).then_inc(S("act_step"), 1)
            act.wait_ge(S("act_step"), nth("act_step"))
            A_(sp_e, sp_e, ACT.Ln, bias=ones[:, 0:1]).then_inc(S("sp_out"), 1)
            for i in range(3):
                act.wait_ge(product_ready, made("lat", i))
                A_(latT[:, 2 * i:2 * i + 2, :].rearrange("p k t -> p (k t)"), at("lat", i)[:, :],
                   ACT.Copy).then_inc(bank_free("lat", i), 1)
            act.wait_ge(S("angles"), nth("angles"))
            A_(sm2[:, 0:32], red, ACT.Sin).then_inc(S("sines"), 1)
            for i in range(12):
                act.wait_ge(S("conv"), nth("conv"))
                A_(qkvT[:, 2 * i:2 * i + 2, :].rearrange("p k t -> p (k t)"), cv[:, i % 2, :],
                                     ACT.Silu).then_inc(bank_free("qkv", i), 1)
            act.wait_ge(product_ready, made("gcum"))
            A_(ngc, at("gcum")[:, 0:PROB], ACT.Copy, scale=-1.0)
            A_(beg, at("gcum")[:, 0:PROB], ACT.Exp).then_inc(bank_free("gcum"), 1)

            def l2_square(i):
                if i >= 2:
                    act.wait_ge(product_ready, made("l2", i - 2))
                A_(sq[:, (i % 2) * 512:(i % 2 + 1) * 512],
                   qkvT[:, 2 * i:2 * i + 2, :].rearrange("p k t -> p (k t)"), ACT.Square)\
                    .then_inc(S("l2_squares"), 1)

            for i in range(12):
                act.wait_ge(bank_free("qkv", i), used("qkv", i))
            l2_square(0)
            for i in range(8):
                if i + 1 < 8:
                    l2_square(i + 1)
                act.wait_ge(product_ready, made("l2", i))
                if i >= 2:
                    act.wait_ge(S("l2_normed"), i - 1)
                A_(rs[:, i % 2, :], at(("l2", i))[:, :], ACT.Ln, bias=eps).then_inc(bank_free("l2", i), 1)
                act.wait_ge(bank_free("l2", i), used("l2", i))
                A_(rs[:, i % 2, :], rs[:, i % 2, :], ACT.Exp, scale=-0.5).then_inc(S("l2_root"), 1)
            for q in range(4):
                act.wait_ge(S("grow_masked"), nth("grow_masked"))
                if q >= 2:
                    A_(eg[:, (q - 2) * 4:(q - 1) * 4, :].rearrange("p h i -> p (h i)"), at(("grow", q))[:, :],
                       ACT.Exp)
                for p in range(4):
                    d = decay1[:, q, p * P:(p + 1) * P]
                    m = A_(d, d, ACT.Exp, bias=ngc[:, q * 4 + p:q * 4 + p + 1])
                    if p == 0:
                        m.then_inc(bank_free("grow", q), 1)
                m.then_inc(S("decays"), 1)
            gates = iter(range(12))

            def fill_gate():
                i = next(gates, None)
                if i is not None:
                    act.wait_ge(product_ready, made("gates", i))
                    A_((gateT, gA, gB)[i // 4][:, 2 * (i % 4):2 * (i % 4) + 2, :]
                             .rearrange("p k t -> p (k t)"), at("gates", i)[:, :],
                       ACT.Silu if i < 4 else ACT.Sigmoid).then_inc(bank_free("gates", i), 1)

            fill_gate()
            fill_gate()
            for s in range(1, LEVELS):
                for q in range(4):
                    if q >= 2 or s > 1:
                        act.wait_ge(product_ready, made(("YT", s, q - 2) if q >= 2 else ("YT", s - 1, q + 2)))
                    act.wait_ge(product_ready, made("Y", s, q))
                    A_(Y[:, q % 2, :], at("Y", s, q)[:, :],
                       ACT.Copy).then_inc(bank_free("Y", s, q), 1)
                fill_gate()
                fill_gate()
            for hq in range(2):
                act.wait_ge(product_ready, made("vn", hq))
                A_(vb[:, hq * 4:hq * 4 + 4, :].rearrange("p h d -> p (h d)"), at("vn", hq)[:, :],
                   ACT.Copy).then_inc(bank_free("vn", hq), 1)
            for hq in range(2):
                act.wait_ge(product_ready, made("S", hq))
                A_(St[:, hq * 4:hq * 4 + 4, :].rearrange("p h d -> p (h d)"), at("S", hq)[:, :],
                   ACT.Copy).then_inc(bank_free("S", hq), 1)
            for hq in range(2):
                act.wait_ge(product_ready, made("vn", 2 + hq))
                A_(vb[:, 8 + hq * 4:12 + hq * 4, :].rearrange("p h d -> p (h d)"), at("vn", 2 + hq)[:, :],
                   ACT.Copy).then_inc(bank_free("vn", 2 + hq), 1)
            for hp in range(4):
                act.wait_ge(product_ready, made("oa", hp))
                A_(sq[:, hp * 512:(hp + 1) * 512], at(("oa", hp))[:, :], ACT.Square).then_inc(S("oa_squares"), 1)
            for hp in range(4):
                act.wait_ge(product_ready, made("oan", hp))
                if hp >= 2:
                    act.wait_ge(S("oa_done"), hp - 1)
                A_(rs[:, hp % 2, :], at(("oan", hp))[:, :], ACT.Ln, bias=eps, scale=1.0 / P).then_inc(bank_free("oan", hp), 1)
                act.wait_ge(bank_free("oan", hp), used("oan", hp))
                A_(rs[:, hp % 2, :], rs[:, hp % 2, :], ACT.Exp, scale=-0.5).then_inc(S("oa_root"), 1)
            A_(sq[:, 0:5 * SEQ], latT[:, 0:5, :].rearrange("p k t -> p (k t)"), ACT.Square)\
                .then_inc(S("lat_squares"), 1)
            act.wait_ge(product_ready, made("latn"))
            act.wait_ge(S("oa_done"), 4)
            A_(rs[:, 0, 0:SEQ], at("latn")[:, 0:SEQ], ACT.Ln, bias=eps, scale=1.0 / Q_RANK)
            A_(rs[:, 0, SEQ:512], at("latn")[:, SEQ:512], ACT.Ln, bias=eps, scale=1.0 / KV_RANK).then_inc(bank_free("latn"), 1)
            act.wait_ge(bank_free("latn"), used("latn"))
            A_(rs[:, 0, :], rs[:, 0, :], ACT.Exp, scale=-0.5).then_inc(S("lat_root"), 1)
            for g in range(4):
                act.wait_ge(product_ready, made("uq", g))
                A_(qnT[:, 2 * g:2 * g + 2, :].rearrange("p k t -> p (k t)"), at("uq", g)[:, :],
                   ACT.Copy).then_inc(bank_free("uq", g), 1)
            for g in range(2):
                act.wait_ge(product_ready, made("uq", 4 + g))
                A_(cv[:, g, :], at("uq", 4 + g)[:, :],
                   ACT.Copy).then_inc(bank_free("uq", 4 + g), 1)
            for g in range(4):
                act.wait_ge(product_ready, made("uk", g))
                A_(knT[:, 2 * g:2 * g + 2, :].rearrange("p k t -> p (k t)"), at("uk", g)[:, :],
                   ACT.Copy).then_inc(bank_free("uk", g), 1)
            for g in range(4):
                act.wait_ge(product_ready, made("uv", g))
                A_(v_tok[:, g // 2, (g % 2) * 512:(g % 2 + 1) * 512], at("uv", g)[:, :],
                   ACT.Copy).then_inc(bank_free("uv", g), 1)

            def attention(name, heads, out_of, sink, sc, PT):
                def exps(h):
                    act.wait_ge(S(name + "_max"), nth(name + "_max"))
                    st = stat[:, h, :]
                    A_(sc[:, h % 2, 0:P], sc[:, h % 2, 0:P], ACT.Exp, bias=st[:, 2:3], accum_out=st[:, 4:5])
                    if sink:
                        A_(st[:, 6:8], st[:, 2:4], ACT.Exp, bias=row("sinks")[:, h:h + 1])
                    A_(sc[:, h % 2, P:384], sc[:, h % 2, P:384], ACT.Exp, bias=st[:, 3:4], accum_out=st[:, 5:6])\
                        .then_inc(S(name + "_exp"), 1)

                exps(0)
                for h in range(heads):
                    if h + 1 < heads:
                        exps(h + 1)
                    if h >= 2:
                        act.wait_ge(product_ready, made(name + "_o", h - 2))
                    act.wait_ge(product_ready, made(name + "_pt", h))
                    A_(PT[:, h % 2, :], at(name + "_pt", h)[:, 0:384],
                       ACT.Copy).then_inc(bank_free(name + "_pt", h), 1)
                    key = (name + "_o", h)
                    act.wait_ge(product_ready, made(key))
                    dst, src = out_of(h, at(key))
                    A_(dst, src, ACT.Copy).then_inc(bank_free(key), 1)

            attention("mla", HEADS, lambda h, b: (obT[:, h, :], b[:, 0:SEQ]), False, sc1, PT1)
            squares_of_x(*[("out1", i) for i in range(4)])
            root("norm_ffn")
            for i in range(KF):
                act.wait_ge(S("conv"), nth("conv"))
                A_(cv[:, i % 2, 0:SEQ], cv[:, i % 2, 0:SEQ], ACT.Silu).then_inc(bank_free("up1", i), 1)
            squares_of_x(*[("down1", i) for i in range(4)])
            root("norm_final")
            act.wait_ge(S("x_new"), nth("x_new"))
            squares_of_x()
            root("norm1")

            act.wait_ge(S("dt_in"), nth("dt_in"))
            A_(expA2, row("a_log2"), ACT.Exp)
            A_(dt_e, dt_t, ACT.Exp).then_inc(S("act_step"), 1)
            act.wait_ge(S("act_step"), nth("act_step"))
            A_(dt_e, dt_e, ACT.Ln, bias=ones[:, 0:1]).then_inc(S("dt_out"), 1)
            for i in range(12):
                act.wait_ge(S("conv"), nth("conv"))
                for j in range(2):
                    m = A_(xbcT[:, 2 * i + j, :], cv[:, i % 2, j * SEQ:(j + 1) * SEQ], ACT.Silu,
                           bias=col("conv_b", 2 * i + j))
                m.then_inc(bank_free("xbc", i), 1)
            for i in range(8):
                act.wait_ge(product_ready, made("z", i))
                A_(zs[:, :, i * 256:(i + 1) * 256], at("z", i)[:, :].rearrange("p (t n) -> p t n", t=TT),
                   ACT.Silu).then_inc(bank_free("z", i), 1)
            act.wait_ge(product_ready, made("acum"))
            A_(nac, at("acum")[:, 0:64], ACT.Copy, scale=-1.0)
            A_(eac, at("acum")[:, 0:64], ACT.Exp).then_inc(bank_free("acum"), 1)
            for c in range(TT):
                for j in range(4):
                    act.wait_ge(product_ready, made("xt", c, j))
                    A_(xs_tok[:, c, j * 512:(j + 1) * 512], at("xt", c, j)[:, :],
                       ACT.Copy).then_inc(bank_free("xt", c, j), 1)
            act.wait_ge(product_ready, made("bmt"))
            A_(bm_tok[:, :, :].rearrange("p g n -> p (g n)"), at("bmt")[:, :],
               ACT.Copy).then_inc(bank_free("bmt"), 1)
            for c in range(TT):
                act.wait_ge(product_ready, made("cb", c))
                A_(CB[:, c, :], at("cb", c)[:, :],
                   ACT.Copy).then_inc(bank_free("cb", c), 1)
            fills = iter([("att2", i) for i in range(6)])

            def fill2():
                key = next(fills, None)
                if key is not None:
                    act.wait_ge(product_ready, made(key))
                    A_(qkv_tok[:, :, key[1] * 256:(key[1] + 1) * 256], at(key)[:, :].rearrange("p (t n) -> p t n", t=TT),
                       ACT.Copy).then_inc(bank_free(key), 1)

            def ssd_decays(n):
                act.wait_ge(S("arow_masked"), nth("arow_masked"))
                for p in range(4):
                    i = (n // 8) * SSD_HEADS + (n % 8) * 4 + p
                    d = decay2[:, n % 4, p * P:(p + 1) * P]
                    m = A_(d, d, ACT.Exp, bias=nac[:, i:i + 1])
                    if p == 0:
                        m.then_inc(bank_free("arow", n), 1)
                m.then_inc(S("ssd_decays"), 1)

            ssd_decays(0)
            ssd_decays(1)
            for n in range(8):
                if n + 1 < 8:
                    ssd_decays(2 * n + 2)
                    ssd_decays(2 * n + 3)
                fill2()
                if n < 4:
                    act.wait_ge(product_ready, made("st", n))
                    A_(state[:, n, :], at("st", n)[:, :],
                       ACT.Copy).then_inc(bank_free("st", n), 1)
                if n < 6:
                    fill2()
                act.wait_ge(S("yz"), nth("yz"))
                A_(sq[:, 0:512], cv[:, n % 2, :], ACT.Square, accum_out=ssq[:, n:n + 1]).then_inc(S("act_step"), 1)
                act.wait_ge(S("act_step"), nth("act_step"))
                A_(ssq[:, n:n + 1], ssq[:, n:n + 1], ACT.Ln, bias=eps, scale=1.0 / 512).then_inc(S("act_step"), 1)
                act.wait_ge(S("act_step"), nth("act_step"))
                A_(ssq[:, n:n + 1], ssq[:, n:n + 1], ACT.Exp, scale=-0.5).then_inc(S("y_root"), 1)
            for i in range(6):
                act.wait_ge(bank_free("att2", i), used("att2", i))
            A_(qk_sq[:, :, :], qkv_tok[:, :, 0:QK_HEADS * A_DIM], ACT.Square).then_inc(S("qk_squares"), 1)
            act.wait_ge(S("qk_sums"), nth("qk_sums"))
            A_(qk_r, qk_ss, ACT.Ln, bias=eps, scale=1.0 / A_DIM).then_inc(S("act_step"), 1)
            act.wait_ge(S("act_step"), nth("act_step"))
            A_(qk_r, qk_r, ACT.Exp, scale=-0.5).then_inc(S("qk_root"), 1)
            for i in range(8):
                act.wait_ge(product_ready, made("gates2", i))
                A_((gA, gB)[i // 4][:, 2 * (i % 4):2 * (i % 4) + 2, :]
                         .rearrange("p k t -> p (k t)"), at("gates2", i)[:, :],
                   ACT.Sigmoid).then_inc(bank_free("gates2", i), 1)
            for j in range(4):
                act.wait_ge(product_ready, made("qt2", j))
                A_(qT2[:, 2 * j:2 * j + 2, :].rearrange("p k t -> p (k t)"), at("qt2", j)[:, :],
                   ACT.Copy).then_inc(bank_free("qt2", j), 1)
            for j in range(2):
                act.wait_ge(product_ready, made("kt2", j))
                A_(kT2[:, 2 * j:2 * j + 2, :].rearrange("p k t -> p (k t)"), at("kt2", j)[:, :],
                   ACT.Copy).then_inc(bank_free("kt2", j), 1)

            def swa_out(h, b):
                lo = (h % 2) * A_DIM
                return oswT[lo:lo + A_DIM, h // 2, :], b[lo:lo + A_DIM, 0:SEQ]

            attention("swa", A_HEADS, swa_out, True, sc2, PT2)
            squares_of_x(*[("out2", i) for i in range(4)])
            root("norm2")
            act.wait_ge(S("group_max"), nth("group_max"))
            for t in range(TT):
                m = A_(rt[:, t, 72:80], rt[:, t, 0:8], ACT.Exp, bias=rt[:, t, 400:401], accum_out=rt[:, t, 401:402])
            m.then_inc(S("group_exp"), 1)
            for n in range(4):
                act.wait_ge(product_ready, made("h2t", n))
                A_(h2_tok[:, n // 2, (n % 2) * 512:(n % 2 + 1) * 512], at("h2t", n)[:, :],
                   ACT.Copy).then_inc(bank_free("h2t", n), 1)
            act.wait_ge(S("top2"), nth("top2"))
            for t in range(TT):
                m = A_(rt[:, t, 402:403], rt[:, t, 403:404], ACT.Exp)
            m.then_inc(S("top2_exp"), 1)
            for k in range(4):
                act.wait_ge(product_ready, made("gather", k))
                A_(xg[:, 2 * k:2 * k + 2, :].rearrange("p k s -> p (k s)"), at("gather", k)[:, 0:2 * P],
                   ACT.Copy).then_inc(bank_free("gather", k), 1)
            with act.Fori(0, GROUPS) as i:
                for name, n in ROUND:
                    b, free = bank[round_bank(name, n)], free_sem[round_bank(name, n)]
                    if name == "gate":
                        act.wait_ge(product_ready, round_made(i, name, n))
                        A_(hid_t[:, n, :], b[:, 0:P], ACT.Silu).then_inc(free, 1)
                    elif name == "turn":
                        act.wait_ge(product_ready, round_made(i, name, n))
                        A_(hidT[:, n, :], b[:, 0:P], ACT.Copy).then_inc(free, 1)
                    elif name == "gather_next":
                        act.wait_ge(product_ready, round_made(i, name, n))
                        A_(xg[:, 2 * n:2 * n + 2, :].rearrange("p k s -> p (k s)"), b[:, 0:2 * P],
                           ACT.Copy).then_inc(free, 1)
                    elif name == "down":
                        act.wait_ge(product_ready, round_made(i, name, n))
                        A_(y_slot[:, n * 512:(n + 1) * 512], b[:, :], ACT.Copy).then_inc(free, 1)

        @block.vector
        def _(dve):
            nth = counter()
            v = nc.vector



            def stt(dst, a, scalar, b, op0=ALU.mult, op1=ALU.mult):
                return v.scalar_tensor_tensor(out=dst, in0=a, scalar=scalar, in1=b, op0=op0, op1=op1)

            def tt(dst, a, b, op):
                return v.tensor_tensor(dst, a, b, op)

            def mul(dst, a, b):
                return v.tensor_tensor(dst, a, b, ALU.mult)

            def add(dst, a, b):
                return v.tensor_tensor(dst, a, b, ALU.add)

            def ts(dst, a, s1, s2=None, op0=ALU.mult, op1=None):
                if op1 is None:
                    return v.tensor_scalar(dst, a, s1, None, op0)
                return v.tensor_scalar(dst, a, s1, s2, op0, op1)

            def norm(gain, dst):
                dve.wait_ge(S("rs_ready"), nth("rs_ready"))
                for k in range(KD):
                    m = stt(dst[:, k, :], xT[:, k, :], col(gain, k), rs[:, 0, 0:SEQ])
                return m

            def conv(key, i, taps, name):
                dve.wait_ge(product_ready, made(key))
                for s_ in range(taps):
                    for j in range(2):
                        w = col(name, (2 * i + j) * taps + taps - 1 - s_)
                        z = at(key)[:, j * SEQ:(j + 1) * SEQ - s_]
                        o = cv[:, i % 2, j * SEQ + s_:(j + 1) * SEQ]
                        m = ts(o, z, w) if s_ == 0 else stt(o, z, w, o, ALU.mult, ALU.add)
                    if s_ < taps - 1:
                        m.then_inc(S("dve_step"), 1)
                        dve.wait_ge(S("dve_step"), nth("dve_step"))
                m.then_inc(S("conv"), 1)

            dve.wait_ge(S("x_landed"), nth("x_landed", 16))
            dve.wait_ge(S("loads"), nth("loads", 64))
            m = norm("norm_mix", hT)
            m.then_inc(S("normed"), 1)
            dve.wait_ge(product_ready, made("ab"))
            pab = at("ab")[:, 0:32].rearrange("p (t n) -> p t n", t=TT)
            z, bb = ab[:, 0:16], ab[:, 16:32]
            v3 = lambda ap: ap.rearrange("p (t n) -> p t n", t=TT)
            add(v3(z), pab[:, :, 0:8], rep(row("dt_bias"), TT, 8))
            v.tensor_copy(v3(bb), pab[:, :, 8:16]).then_inc(bank_free("ab"), 1)
            dve.wait_ge(bank_free("ab"), used("ab"))
            ts(sp_t, z, -1.0).then_inc(S("dve_step"), 1)
            dve.wait_ge(S("dve_step"), nth("dve_step"))
            tt(sp_t, sp_t, z, ALU.min).then_inc(S("sp_in"), 1)
            dve.wait_ge(S("sp_out"), nth("sp_out"))
            stt(sp_t, z, 0.0, sp_e, ALU.max, ALU.add).then_inc(S("dve_step"), 1)
            dve.wait_ge(S("dve_step"), nth("dve_step"))
            stt(v3(glog), v3(sp_t), -1.0, rep(expA, TT, 8))
            ts(bb, bb, 1.0, op0=ALU.add).then_inc(S("dve_step"), 1)
            dve.wait_ge(S("dve_step"), nth("dve_step"))
            v.reciprocal(beta, bb).then_inc(S("glog"), 1)
            dve.wait_ge(S("late_loads"), nth("late_loads", 48))
            v.tensor_copy(pos_f, pos_sb[:, :]).then_inc(S("dve_step"), 1)
            dve.wait_ge(S("dve_step"), nth("dve_step"))
            for t in range(TT):
                m = ts(ang[:, t * 8:(t + 1) * 8], con("inv_freq"), pos_f[:, t:t + 1])
            m.then_inc(S("dve_step"), 1)
            dve.wait_ge(S("dve_step"), nth("dve_step"))
            ts(rnd[:, 0:16], ang, 1.0 / (2 * np.pi))
            ts(rnd[:, 16:32], ang, 1.0 / (2 * np.pi), 0.25, ALU.mult, ALU.add).then_inc(S("dve_step"), 1)
            dve.wait_ge(S("dve_step"), nth("dve_step"))
            magic = 1.5 * 2.0 ** 23
            ts(rnd, rnd, magic, op0=ALU.add).then_inc(S("dve_step"), 1)
            dve.wait_ge(S("dve_step"), nth("dve_step"))
            ts(rnd, rnd, -magic, op0=ALU.add).then_inc(S("dve_step"), 1)
            dve.wait_ge(S("dve_step"), nth("dve_step"))
            c1, c2 = 6.28125, float(np.float32(1.93500518798828125e-3))
            c3 = 2 * np.pi - c1 - c2
            stt(red[:, 0:16], rnd[:, 0:16], -c1, ang, ALU.mult, ALU.add)
            stt(red[:, 16:32], rnd[:, 16:32], -c1, ang, ALU.mult, ALU.add).then_inc(S("dve_step"), 1)
            dve.wait_ge(S("dve_step"), nth("dve_step"))
            stt(red, rnd, -c2, red, ALU.mult, ALU.add).then_inc(S("dve_step"), 1)
            dve.wait_ge(S("dve_step"), nth("dve_step"))
            stt(red, rnd, -c3, red, ALU.mult, ALU.add).then_inc(S("dve_step"), 1)
            dve.wait_ge(S("dve_step"), nth("dve_step"))
            ts(red[:, 16:32], red[:, 16:32], np.pi / 2, op0=ALU.add).then_inc(S("dve_step"), 1)
            dve.wait_ge(S("dve_step"), nth("dve_step"))
            top = 3.1415925
            ts(red, red, top, -top, ALU.min, ALU.max).then_inc(S("angles"), 1)
            for i in range(12):
                if i >= 2:
                    dve.wait_ge(bank_free("qkv", i - 2), used("qkv", i - 2))
                conv(("qkv", i), i, 4, "conv_qkv")
            dve.wait_ge(bank_free("qkv", 10), used("qkv", 10))
            dve.wait_ge(bank_free("qkv", 11), used("qkv", 11))
            dve.wait_ge(bank_free("gcum"), used("gcum"))
            mul(beg, beg, beta)
            for i in range(8):
                dve.wait_ge(S("l2_root"), nth("l2_root"))
                pair = qkvT[:, 2 * i:2 * i + 2, :].rearrange("p k t -> p (k t)")
                stt(pair, pair, float(P) ** -0.5 if i < 4 else 1.0, rs[:, i % 2, :]).then_inc(S("l2_normed"), 1)
            dve.wait_ge(product_ready, made("vt", 3))
            for n in range(4):
                key = ("vt", n)
                mul(vb[:, n * 4:n * 4 + 4, :], quads(at(key)[:, :]), b3(beta[:, n * 4:n * 4 + 4], 4, P)).then_inc(bank_free(key), 1)

            def mask_decays(q):
                dve.wait_ge(product_ready, made("grow", q))
                add(quads(decay1[:, q, :]), quads(at(("grow", q))[:, :]), rep(con("neg_late"), 4, P))\
                    .then_inc(S("grow_masked"), 1)

            mask_decays(0)
            for q in range(4):
                dve.wait_ge(S("decays"), nth("decays"))
                dec = quads(decay1[:, q, :])
                if q < 2:
                    v.tensor_copy(kds[:, q * 4:q * 4 + 4], dec[:, :, P - 1]).then_inc(S("dve_step"), 1)
                    dve.wait_ge(S("dve_step"), nth("dve_step"))
                    dve.wait_ge(product_ready, made("kt", q))
                    mul(kd[:, q * 4:q * 4 + 4, :], quads(at(("kt", q))[:, :]),
                                         b3(kds[:, q * 4:q * 4 + 4], 4, P)).then_inc(bank_free("kt", q), 1)
                if q + 1 < 4:
                    mask_decays(q + 1)
                four = slice(q * 4, q * 4 + 4)
                dve.wait_ge(product_ready, made("gram", q))
                mul(LT[:, four, :], quads(at(("gram", q))[:, :]), dec).then_inc(bank_free("gram", q), 1)
                dve.wait_ge(bank_free("gram", q), used("gram", q))
                mul(LT[:, four, :], LT[:, four, :], quads(at(("brow", q))[:, :])).then_inc(bank_free("brow", q), 1)
                dve.wait_ge(product_ready, made("qk", q))
                mul(AT[:, four, :], quads(at(("qk", q))[:, :]), dec).then_inc(bank_free("qk", q), 1)
            dve.wait_ge(bank_free("grow", 3), used("grow", 3))
            dve.wait_ge(bank_free("brow", 3), used("brow", 3))
            mul(qkvT[:, 0:HEADS, P:SEQ], qkvT[:, 0:HEADS, P:SEQ], eg[:, :, :]).then_inc(S("q_decayed"), 1)

            def off_diagonal(s_, q):
                return mul(quads(BT[:, q % 2, :]), LT[:, q * 4:q * 4 + 4, :], rep(levels[:, s_, :], 4, P))\
                    .then_inc(S("off_diagonal"), 1)

            def first_t(q):
                dve.wait_ge(product_ready, made("Y", 0, q))
                tt(T[:, q * 4:q * 4 + 4, :], rep(ident, 4, P), quads(at(("Y", 0, q))[:, :]),
                                      ALU.subtract).then_inc(bank_free("Y", 0, q), 1)

            for q in range(4):
                if q >= 2:
                    dve.wait_ge(product_ready, made("Y", 0, q - 2))
                off_diagonal(0, q)
                dve.wait_ge(S("off_diagonal"), nth("off_diagonal"))
                tt(TTr[:, q * 4:q * 4 + 4, :], rep(ident, 4, P), quads(BT[:, q % 2, :]), ALU.subtract).then_inc(S("dve_step"), 1)
                dve.wait_ge(S("dve_step"), nth("dve_step"))
                if q >= 1:
                    first_t(q - 1)
            first_t(3)
            for s_ in range(1, LEVELS):
                for q in range(4):
                    dve.wait_ge(product_ready, made(("Y", s_, q - 2) if q >= 2 else ("Y", s_ - 1, q + 2)))
                    off_diagonal(s_, q)
                for q in range(4):
                    four = slice(q * 4, q * 4 + 4)
                    for key, dst in (("TY", T), ("YT", TTr)) if s_ < LEVELS - 1 else (("YT", TTr),):
                        k = (key, s_, q)
                        dve.wait_ge(product_ready, made(k))
                        if key == "TY":
                            dve.wait_ge(product_ready, made("YT", s_, q))
                        tt(dst[:, four, :], dst[:, four, :], quads(at(k)[:, :]), ALU.subtract).then_inc(bank_free(k), 1)
            for hq in range(2):
                key = ("KS", hq)
                dve.wait_ge(product_ready, made(key))
                mul(quads(tmp[:, hq, :]), quads(at(key)[:, :]),
                                    b3(beg[:, 8 + hq * 4:12 + hq * 4], 4, P)).then_inc(bank_free(key), 1)
                dve.wait_ge(bank_free(key), used(key))
                r = vb[:, 8 + hq * 4:12 + hq * 4, :]
                tt(r, r, quads(tmp[:, hq, :]), ALU.subtract).then_inc(S("residual"), 1)
            for i in range(12):
                dve.wait_ge(bank_free("gates", i), used("gates", i))
            for hp in range(4):
                dve.wait_ge(S("oa_root"), nth("oa_root"))
                key, pair = ("oa", hp), oaT[:, 2 * hp:2 * hp + 2, :].rearrange("p k t -> p (k t)")
                stt(pair, at(key)[:, :], col("gdn_norm"), rs[:, hp % 2, :]).then_inc(bank_free(key), 1)
                dve.wait_ge(bank_free(key), used(key))
                mul(pair, pair, gateT[:, 2 * hp:2 * hp + 2, :].rearrange("p k t -> p (k t)"))\
                    .then_inc(S("oa_done"), 1)
            dve.wait_ge(S("lat_root"), nth("lat_root"))
            for k in range(KQ):
                stt(latT[:, k, :], latT[:, k, :], col("mla_q", k), rs[:, 0, 0:SEQ])
            for k in range(KKV):
                m = stt(latT[:, KQ + k, :], latT[:, KQ + k, :], col("mla_kv", k), rs[:, 0, SEQ:512])
            m.then_inc(S("lat_normed"), 1)
            dve.wait_ge(product_ready, made("krot"))
            mul(latT[:, 5, :], latT[:, 5, :], con("rope_cos"))
            mul(tmp[:, 0, 0:SEQ], at("krot")[:, 0:SEQ], con("rope_sin")).then_inc(bank_free("krot"), 1)
            dve.wait_ge(bank_free("krot"), used("krot"))
            add(latT[:, 5, :], latT[:, 5, :], tmp[:, 0, 0:SEQ]).then_inc(S("dve_step"), 1)
            dve.wait_ge(S("dve_step"), nth("dve_step"))
            for g in range(2):
                key = ("qrot", g)
                dve.wait_ge(product_ready, made(key))
                pair = qpeT[:, 2 * g:2 * g + 2, :]
                mul(pair, quads(cv[:, g, :], 2), rep(con("rope_cos"), 2, SEQ))
                mul(quads(tmp[:, g, :], 2), quads(at(key)[:, :], 2), rep(con("rope_sin"), 2, SEQ)).then_inc(bank_free(key), 1)
                dve.wait_ge(bank_free(key), used(key))
                m = add(pair, pair, quads(tmp[:, g, :], 2))
            m.then_inc(S("mla_in"), 1)

            def attention(name, heads, scale, mask, sink, sc):
                def maxima(h):
                    key = (name + "_s", h)
                    dve.wait_ge(product_ready, made(key))
                    if h >= 2:
                        dve.wait_ge(product_ready, made(name + "_pt", h - 2))
                    st, s_ = stat[:, h, :], sc[:, h % 2, :]
                    stt(s_, at(key)[:, 0:384], scale, con(mask), ALU.mult, ALU.add).then_inc(bank_free(key), 1)
                    dve.wait_ge(bank_free(key), used(key))
                    v.tensor_reduce(st[:, 0:1], s_[:, 0:P], AX.X, ALU.max)
                    v.tensor_reduce(st[:, 1:2], s_[:, P:384], AX.X, ALU.max).then_inc(S("dve_step"), 1)
                    dve.wait_ge(S("dve_step"), nth("dve_step"))
                    if sink:
                        ts(st[:, 0:2], st[:, 0:2], row("sinks")[:, h:h + 1], op0=ALU.max).then_inc(S("dve_step"), 1)
                        dve.wait_ge(S("dve_step"), nth("dve_step"))
                    ts(st[:, 2:4], st[:, 0:2], -1.0).then_inc(S(name + "_max"), 1)

                maxima(0)
                for h in range(heads):
                    if h + 1 < heads:
                        maxima(h + 1)
                    dve.wait_ge(S(name + "_exp"), nth(name + "_exp"))
                    st = stat[:, h, :]
                    if sink:
                        add(st[:, 4:6], st[:, 4:6], st[:, 6:8]).then_inc(S("dve_step"), 1)
                        dve.wait_ge(S("dve_step"), nth("dve_step"))
                    v.reciprocal(st[:, 8:10], st[:, 4:6]).then_inc(S("dve_step"), 1)
                    dve.wait_ge(S("dve_step"), nth("dve_step"))
                    ts(sc[:, h % 2, 0:P], sc[:, h % 2, 0:P], st[:, 8:9])
                    ts(sc[:, h % 2, P:384], sc[:, h % 2, P:384], st[:, 9:10]).then_inc(S(name + "_p"), 1)

            def merge(first, second, out_, merged):
                for i in range(4):
                    pair = slice(2 * i, 2 * i + 2)
                    dve.wait_ge(product_ready, made(first, i))
                    mul(merged[:, pair, :], quads(at((first, i))[:, :], 2), gA[:, pair, :]).then_inc(bank_free(first, i), 1)
                for i in range(4):
                    pair = slice(2 * i, 2 * i + 2)
                    dve.wait_ge(product_ready, made(second, i))
                    if i >= 2:
                        dve.wait_ge(S("merged"), nth("merged"))
                    mul(quads(tmp[:, i % 2, :], 2), quads(at((second, i))[:, :], 2),
                                                gB[:, pair, :]).then_inc(bank_free(second, i), 1)
                    dve.wait_ge(bank_free(second, i), used(second, i))
                    add(merged[:, pair, :], merged[:, pair, :], quads(tmp[:, i % 2, :], 2)).then_inc(S("merged"), 1)
                dve.wait_ge(S("merged"), nth("merged", 2))
                residual(out_)

            def residual(name):
                for i in range(4):
                    pair = slice(2 * i, 2 * i + 2)
                    dve.wait_ge(product_ready, made(name, i))
                    add(xT[:, pair, :], xT[:, pair, :], quads(at((name, i))[:, :], 2)).then_inc(bank_free(name, i), 1)

            attention("mla", HEADS, MLA_SCALE, "mla_mask", False, sc1)
            merge("o_gdn", "o_mla", "out1", mergedT)
            norm("norm_ffn", hT).then_inc(S("normed"), 1)

            def ffn_product(i):
                dve.wait_ge(bank_free("up1", i), used("up1", i))
                mul(ffT[:, i, :], cv[:, i % 2, 0:SEQ], cv[:, i % 2, SEQ:512]).then_inc(S("ff"), 1)

            for i in range(KF):
                if i >= 2:
                    dve.wait_ge(S("ff"), nth("ff"))
                conv(("up1", i), i, 3, "conv_ffn")
                if i >= 1:
                    ffn_product(i - 1)
            ffn_product(KF - 1)
            residual("down1")
            norm("norm_final", xT).then_inc(S("x_new"), 1)
            norm("norm1", hT).then_inc(S("normed"), 1)

            dve.wait_ge(product_ready, made("dt"))
            v32 = lambda ap: ap.rearrange("p (t n) -> p t n", t=TT)
            add(v32(dt_), v32(at("dt")[:, 0:64]), rep(row("dt_bias2"), TT, 32)).then_inc(bank_free("dt"), 1)
            dve.wait_ge(bank_free("dt"), used("dt"))
            ts(dt_t, dt_, -1.0).then_inc(S("dve_step"), 1)
            dve.wait_ge(S("dve_step"), nth("dve_step"))
            tt(dt_t, dt_t, dt_, ALU.min).then_inc(S("dt_in"), 1)
            dve.wait_ge(S("dt_out"), nth("dt_out"))
            stt(dt_, dt_, 0.0, dt_e, ALU.max, ALU.add).then_inc(S("dve_step"), 1)
            dve.wait_ge(S("dve_step"), nth("dve_step"))
            stt(v32(dA), v32(dt_), -1.0, rep(expA2, TT, 32)).then_inc(S("dA"), 1)
            for i in range(12):
                if i >= 2:
                    dve.wait_ge(bank_free("xbc", i - 2), used("xbc", i - 2))
                conv(("xbc", i), i, 4, "conv2")
            dve.wait_ge(bank_free("xbc", 10), used("xbc", 10))
            dve.wait_ge(bank_free("xbc", 11), used("xbc", 11))
            for i in range(8):
                dve.wait_ge(bank_free("z", i), used("z", i))
            dve.wait_ge(bank_free("acum"), used("acum"))
            by_head = lambda ap: ap.rearrange("p (h d) -> p h d", d=64)
            dve.wait_ge(bank_free("cb", 0), used("cb", 0))
            dve.wait_ge(bank_free("cb", 1), used("cb", 1))

            def mask_rows(n):
                dve.wait_ge(product_ready, made("arow", n))
                if n >= 4:
                    dve.wait_ge(product_ready, made("y", (n - 4) // 2))
                add(quads(decay2[:, n % 4, :]), quads(at(("arow", n))[:, :]), rep(con("neg_late"), 4, P))\
                    .then_inc(S("arow_masked"), 1)

            def ssd_product(n):
                dve.wait_ge(S("ssd_decays"), nth("ssd_decays"))
                c, g = n // 8, n % 8 // 2
                dec = quads(decay2[:, n % 4, :])
                if c == 0:
                    v.tensor_copy(de[:, n * 4:n * 4 + 4], dec[:, :, P - 1]).then_inc(S("dve_step"), 1)
                    dve.wait_ge(S("dve_step"), nth("dve_step"))
                mul(dec, dec, rep(CB[:, c, g * P:(g + 1) * P], 4, P)).then_inc(S("decay_mult"), 1)

            def y_norm(n):
                dve.wait_ge(S("y_root"), nth("y_root"))
                ts(cv[:, n % 2, :], cv[:, n % 2, :], ssq[:, n:n + 1]).then_inc(S("y_normed"), 1)

            def y_turned(n):
                c, g = n // 4, n % 4
                dve.wait_ge(product_ready, made("ynt", n))
                mul(ysT[:, g * 4:g * 4 + 4, c * P:(c + 1) * P], quads(at(("ynt", n))[:, :]),
                                      b3(col("ssd_norm", g * 4, 4), 4, P)).then_inc(bank_free("ynt", n), 1)

            mask_rows(0)
            mask_rows(1)
            for n in range(8):
                c, g = n // 4, n % 4
                part = slice(g * 512, (g + 1) * 512)
                if n + 1 < 8:
                    mask_rows(2 * n + 2)
                    mask_rows(2 * n + 3)
                if n >= 2:
                    dve.wait_ge(product_ready, made("y", n - 2))
                dve.wait_ge(bank_free("xt", c, g), used("xt", c, g))
                mul(by_head(xdt[:, n % 2, :]), by_head(xs_tok[:, c, part]),
                         b3(dt_[:, c * 32 + g * 8:c * 32 + g * 8 + 8], 8, 64)).then_inc(S("dve_step"), 1)
                dve.wait_ge(S("dve_step"), nth("dve_step"))
                ssd_product(2 * n)
                ssd_product(2 * n + 1)
                if c == 0:
                    if g >= 2:
                        dve.wait_ge(product_ready, made("st", g - 2))
                    mul(by_head(xde[:, g % 2, :]), by_head(xdt[:, n % 2, :]), b3(de[:, g * 8:g * 8 + 8], 8, 64))\
                        .then_inc(S("xde"), 1)
                if n >= 1:
                    y_norm(n - 1)
                if n >= 2:
                    dve.wait_ge(product_ready, made("ynt", n - 2))
                y = cv[:, n % 2, :]
                mul(by_head(y), by_head(xs_tok[:, c, part]), b3(row("d_skip")[:, g * 8:g * 8 + 8], 8, 64)).then_inc(S("dve_step"), 1)
                dve.wait_ge(S("dve_step"), nth("dve_step"))
                dve.wait_ge(product_ready, made("y", n))
                add(y, y, at(("y", n))[:, :]).then_inc(bank_free("y", n), 1)
                dve.wait_ge(bank_free("y", n), used("y", n))
                if c == 1:
                    dve.wait_ge(product_ready, made("yo", g))
                    mul(by_head(tmp[:, 0, :]), by_head(at(("yo", g))[:, :]),
                                              b3(eac[:, 32 + g * 8:40 + g * 8], 8, 64)).then_inc(bank_free("yo", g), 1)
                    dve.wait_ge(bank_free("yo", g), used("yo", g))
                    add(y, y, tmp[:, 0, :]).then_inc(S("dve_step"), 1)
                    dve.wait_ge(S("dve_step"), nth("dve_step"))
                mul(y, y, zs[:, c, part]).then_inc(S("yz"), 1)
                if n >= 1:
                    y_turned(n - 1)
            y_norm(7)
            y_turned(7)

            dve.wait_ge(S("qk_squares"), nth("qk_squares"))
            v.tensor_reduce(qk_ss, qk_sq[:, :, :].rearrange("p t (h d) -> p (t h) d", d=A_DIM), AX.X, ALU.add)\
                .then_inc(S("qk_sums"), 1)
            dve.wait_ge(S("qk_root"), nth("qk_root"))
            dve.wait_ge(S("sines"), nth("sines"))
            heads_of = lambda t, h0, h1: qkv_tok[:, t, h0 * A_DIM:h1 * A_DIM].rearrange("p (h d) -> p h d", d=A_DIM)
            for t in range(TT):
                w = heads_of(t, 0, QK_HEADS)
                m = mul(w, w, b3(qk_r[:, t * QK_HEADS:(t + 1) * QK_HEADS], QK_HEADS, A_DIM))
            m.then_inc(S("dve_step"), 1)
            dve.wait_ge(S("dve_step"), nth("dve_step"))
            for t in range(TT):
                for h0, h1, gain in ((0, A_HEADS, "q_gain"), (A_HEADS, QK_HEADS, "k_gain")):
                    w = heads_of(t, h0, h1)
                    m = mul(w, w, rep(row(gain), h1 - h0, A_DIM))
            m.then_inc(S("dve_step"), 1)
            dve.wait_ge(S("dve_step"), nth("dve_step"))
            halves = []
            for t in range(TT):
                w = heads_of(t, 0, QK_HEADS)
                x1, x2 = w[:, :, 0:8], w[:, :, 8:16]
                cs, sn = (rep(a[:, t * 8:(t + 1) * 8], QK_HEADS, 8) for a in (cos2, sin2))
                r = [rope_t[:, n, t * QK_HEADS * 8:(t + 1) * QK_HEADS * 8].rearrange("p (h d) -> p h d", d=8)
                     for n in range(4)]
                mul(r[0], x1, cs)
                mul(r[1], x2, sn)
                mul(r[2], x2, cs)
                m = mul(r[3], x1, sn)
                halves.append((x1, x2, r))
            m.then_inc(S("dve_step"), 1)
            dve.wait_ge(S("dve_step"), nth("dve_step"))
            for x1, x2, r in halves:
                tt(x1, r[0], r[1], ALU.subtract)
                m = add(x2, r[2], r[3])
            m.then_inc(S("dve_step"), 1)
            dve.wait_ge(S("dve_step"), nth("dve_step"))
            for t in range(TT):
                for half in range(2):
                    m = v.tensor_copy(kdup[:, t, :, half * A_DIM:(half + 1) * A_DIM], heads_of(t, A_HEADS, QK_HEADS))
            m.then_inc(S("q_tok2"), 1)
            for i in range(8):
                dve.wait_ge(bank_free("gates2", i), used("gates2", i))
            attention("swa", A_HEADS, ATT_SCALE, "swa_mask", True, sc2)
            merge("o_ssd", "o_swa", "out2", merged2T)
            norm("norm2", hT).then_inc(S("normed"), 1)

            dve.wait_ge(product_ready, made("route"))
            add(rt[:, :, 0:72], at("route")[:, 0:144].rearrange("p (t n) -> p t n", t=TT),
                                    rep(row("b_router"), TT, 72)).then_inc(bank_free("route"), 1)
            dve.wait_ge(bank_free("route"), used("route"))
            both = range(TT)


            for t in both:
                m = v.max(rt[:, t, 80:88], rt[:, t, 0:8])
            m.then_inc(S("dve_step"), 1)
            dve.wait_ge(S("dve_step"), nth("dve_step"))
            for t in both:
                m = ts(rt[:, t, 400:401], rt[:, t, 80:81], -1.0)
            m.then_inc(S("group_max"), 1)
            for t in both:
                m = v.max_index(ridx[:, t, 0:8], rt[:, t, 80:88], rt[:, t, 0:8])
            m.then_inc(S("dve_step"), 1)
            dve.wait_ge(S("dve_step"), nth("dve_step"))
            for t in both:
                m = v.tensor_copy(rt[:, t, 112:113], ridx[:, t, 0:1])
            m.then_inc(S("dve_step"), 1)
            dve.wait_ge(S("dve_step"), nth("dve_step"))
            for t in both:
                m = ts(rt[:, t, 88:96], con("iota")[:, 0:8], rt[:, t, 112:113], op0=ALU.is_equal)
            m.then_inc(S("dve_step"), 1)
            dve.wait_ge(S("dve_step"), nth("dve_step"))
            for t in both:
                m = mul(rt[:, t, 120:184].rearrange("p (g e) -> p g e", g=EGROUPS),
                               rt[:, t, 8:72].rearrange("p (g e) -> p g e", g=EGROUPS),
                               b3(rt[:, t, 88:96], EGROUPS, EPG))
            m.then_inc(S("dve_step"), 1)
            dve.wait_ge(S("dve_step"), nth("dve_step"))
            for t in both:
                m = v.tensor_reduce(rt[:, t, 96:104], rt[:, t, 120:184].rearrange("p (g e) -> p e g", g=EGROUPS),
                                           AX.X, ALU.add)
            m.then_inc(S("dve_step"), 1)
            dve.wait_ge(S("dve_step"), nth("dve_step"))
            for t in both:
                m = v.max(rt[:, t, 104:112], rt[:, t, 96:104])
            m.then_inc(S("dve_step"), 1)
            dve.wait_ge(S("dve_step"), nth("dve_step"))
            for t in both:
                m = tt(rt[:, t, 403:404], rt[:, t, 105:106], rt[:, t, 104:105], ALU.subtract)
            m.then_inc(S("top2"), 1)
            for t in both:
                m = v.max_index(ridx[:, t, 8:16], rt[:, t, 104:112], rt[:, t, 96:104])
            m.then_inc(S("dve_step"), 1)
            dve.wait_ge(S("dve_step"), nth("dve_step"))
            for t in both:
                m = v.tensor_copy(rt[:, t, 113:115], ridx[:, t, 8:10])
            m.then_inc(S("dve_step"), 1)
            dve.wait_ge(S("dve_step"), nth("dve_step"))
            for k in range(2):
                for t in both:
                    m = stt(rt[:, t, 113 + k:114 + k], rt[:, t, 112:113], float(EPG), rt[:, t, 113 + k:114 + k],
                                   ALU.mult, ALU.add)
                m.then_inc(S("dve_step"), 1)
                dve.wait_ge(S("dve_step"), nth("dve_step"))
            for k in range(2):
                for t in both:
                    m = ts(rt[:, t, 256 + 64 * k:320 + 64 * k], con("iota")[:, 0:64], rt[:, t, 113 + k:114 + k],
                                  op0=ALU.is_equal)
                m.then_inc(S("dve_step"), 1)
                dve.wait_ge(S("dve_step"), nth("dve_step"))
            for t in both:
                m = add(rt[:, t, 192:256], rt[:, t, 256:320], rt[:, t, 320:384])
            m.then_inc(S("chosen"), 1)
            dve.wait_ge(S("group_exp"), nth("group_exp"))
            dve.wait_ge(S("top2_exp"), nth("top2_exp"))
            for t in both:
                m = v.reciprocal(rt[:, t, 404:405], rt[:, t, 401:402])
            m.then_inc(S("dve_step"), 1)
            dve.wait_ge(S("dve_step"), nth("dve_step"))
            for t in both:
                m = ts(rt[:, t, 405:406], rt[:, t, 402:403], 1.0, op0=ALU.add)
            m.then_inc(S("dve_step"), 1)
            dve.wait_ge(S("dve_step"), nth("dve_step"))
            for t in both:
                m = v.reciprocal(rt[:, t, 388:389], rt[:, t, 405:406])
            m.then_inc(S("dve_step"), 1)
            dve.wait_ge(S("dve_step"), nth("dve_step"))
            for t in both:
                m = mul(rt[:, t, 389:390], rt[:, t, 388:389], rt[:, t, 402:403])
            m.then_inc(S("dve_step"), 1)
            dve.wait_ge(S("dve_step"), nth("dve_step"))
            for t in both:
                m = ts(rt[:, t, 388:390], rt[:, t, 388:390], rt[:, t, 404:405])
            m.then_inc(S("dve_step"), 1)
            dve.wait_ge(S("dve_step"), nth("dve_step"))
            dve.wait_ge(product_ready, made("counts"))
            cnt, nblk, incl, start = (rtx[:, 64 * n:64 * n + 64] for n in range(4))
            v.tensor_copy(cnt, at("counts")[:, 0:64]).then_inc(S("dve_step"), 1)
            dve.wait_ge(S("dve_step"), nth("dve_step"))
            ts(nblk, cnt, float(CAP), op0=ALU.is_gt).then_inc(S("dve_step"), 1)
            dve.wait_ge(S("dve_step"), nth("dve_step"))
            for n in range(2, SEQ // CAP):
                stt(nblk, cnt, float(n * CAP), nblk, ALU.is_gt, ALU.add).then_inc(S("dve_step"), 1)
                dve.wait_ge(S("dve_step"), nth("dve_step"))
            v.tensor_tensor_scan(incl, ones[:, 0:64], nblk, 0.0, ALU.mult, ALU.add).then_inc(S("dve_step"), 1)
            dve.wait_ge(S("dve_step"), nth("dve_step"))
            tt(start, incl, nblk, ALU.subtract).then_inc(S("dve_step"), 1)
            dve.wait_ge(S("dve_step"), nth("dve_step"))
            ts(own_to_over, con("iota")[:, 0:64], -float(CAP), float(EXPERTS * CAP - CAP), ALU.mult, ALU.add)\
                .then_inc(S("dve_step"), 1)
            dve.wait_ge(S("dve_step"), nth("dve_step"))
            stt(own_to_over, start, float(CAP), own_to_over, ALU.mult, ALU.add).then_inc(S("dve_step"), 1)
            dve.wait_ge(S("dve_step"), nth("dve_step"))
            for t in both:
                rank = at("counts")[:, 64 + 64 * t:128 + 64 * t]
                stt(rtx[:, 256 + 64 * t:320 + 64 * t], rank, float(CAP), own_to_over, ALU.is_ge, ALU.mult)
                m = stt(rt[:, t, 448:512], con("iota")[:, 0:64], float(CAP), rank, ALU.mult, ALU.add)
            m.then_inc(bank_free("counts"), 1)
            dve.wait_ge(bank_free("counts"), used("counts"))
            for t in both:
                m = add(rt[:, t, 448:512], rt[:, t, 448:512], rtx[:, 256 + 64 * t:320 + 64 * t])
            m.then_inc(S("dve_step"), 1)
            dve.wait_ge(S("dve_step"), nth("dve_step"))
            for k in range(2):
                for t in both:
                    m = mul(rtx[:, 256 + 64 * t:320 + 64 * t], rt[:, t, 448:512],
                                   rt[:, t, 256 + 64 * k:320 + 64 * k])
                m.then_inc(S("dve_step"), 1)
                dve.wait_ge(S("dve_step"), nth("dve_step"))
                for t in both:
                    m = v.tensor_reduce(rt[:, t, 384 + k:385 + k], rtx[:, 256 + 64 * t:320 + 64 * t],
                                               AX.X, ALU.add)
                m.then_inc(S("dve_step"), 1)
                dve.wait_ge(S("dve_step"), nth("dve_step"))
            ts(rtx[:, 384:448], incl, con("part")[:, 0:1], op0=ALU.is_le).then_inc(S("dve_step"), 1)
            dve.wait_ge(S("dve_step"), nth("dve_step"))
            v.tensor_reduce(rtx[:, 512:513], rtx[:, 384:448], AX.X, ALU.add).then_inc(S("places"), 1)
            dve.wait_ge(product_ready, made("be"))
            v.tensor_copy(be_row[:, 0:P], at("be")[0:1, 0:P])
            ts(be_row[:, P:2 * P], at("be")[0:1, 0:P], float(EXPERTS - 1), op0=ALU.min).then_inc(bank_free("be"), 1)
            for key, dst in (("d_row", d_row), ("g_row", g_row)):
                dve.wait_ge(product_ready, made(key))
                v.tensor_copy(dst[:, :, :].rearrange("p k t -> p (k t)"), at(key)[:, :]).then_inc(bank_free(key), 1)
            slot_of = rtx[:, 560:561]
            v.tensor_copy(slot_of, con("part")[:, 0:1]).then_inc(S("dve_step"), 1)
            dve.wait_ge(S("dve_step"), nth("dve_step"))

            def select():
                for t in both:
                    m = ts(sel_t[:, t, :], con("iota"), rt[:, t, 384:385], op0=ALU.is_equal)
                m.then_inc(S("dve_step"), 1)
                dve.wait_ge(S("dve_step"), nth("dve_step"))
                for t in both:
                    m = stt(sel[:, t, :], con("iota"), rt[:, t, 385:386], sel_t[:, t, :], ALU.is_equal, ALU.add)
                m.then_inc(S("sel_ready"), 1)
                dve.wait_ge(S("sel_ready"), nth("sel_ready"))
                ts(rt[:, :, 384:386], rt[:, :, 384:386], -float(P), op0=ALU.add).then_inc(S("dve_step"), 1)
                dve.wait_ge(S("dve_step"), nth("dve_step"))

            select()
            v.memset(y_slot[:, :], 0.0)
            v.memset(selw[:, :], 0.0).then_inc(S("selw_ready"), 1)
            for key in product:
                if key[0] == "pad":
                    dve.wait_ge(product_ready, made(key))
                    v.tensor_copy(rtx[:, 600:601], at(key)[:, 0:1]).then_inc(bank_free(key), 1)
                    dve.wait_ge(bank_free(key), used(key))
            dve.wait_ge(product_ready, made("gather", 3))
            select()
            with dve.Fori(0, GROUPS) as i:
                dve.wait_ge(product_ready, round_made(i, "up", 0))
                dve.wait_ge(free_sem[round_bank("gate", 0)], round_used(i, "gate", 0))
                mul(hid[:, 0, :], hid_t[:, 0, :], bank[round_bank("up", 0)][:, 0:P])\
                    .then_inc(free_sem[round_bank("up", 0)], 1)
                for n in range(4):
                    part = slice(2 * n, 2 * n + 2)
                    dve.wait_ge(product_ready, round_made(i, "scatter_last", n))
                    add(xT[:, part, :], xT[:, part, :], quads(bank[round_bank("scatter_last", n)][:, :], 2))\
                        .then_inc(free_sem[round_bank("scatter_last", n)], 1)
                dve.wait_ge(product_ready, round_made(i, "up", 1))
                dve.wait_ge(free_sem[round_bank("gate", 1)], round_used(i, "gate", 1))
                mul(hid[:, 1, :], hid_t[:, 1, :], bank[round_bank("up", 1)][:, 0:P])\
                    .then_inc(free_sem[round_bank("up", 1)], 1)
                stt(selw[:, :], d_row[:, 0, :], slot_of, g_row[:, 0, :], ALU.is_equal, ALU.mult)
                stt(selw_t[:, :], d_row[:, 1, :], slot_of, g_row[:, 1, :], ALU.is_equal, ALU.mult)\
                    .then_inc(S("round_step"), 1)
                dve.wait_ge(S("round_step"), i * 4 + 1)
                add(selw[:, :], selw[:, :], selw_t[:, :]).then_inc(S("selw_ready"), 1)
                ts(slot_of, slot_of, float(P), op0=ALU.add).then_inc(S("round_step"), 1)
                dve.wait_ge(S("round_step"), i * 4 + 2)
                dve.wait_ge(product_ready, round_made(i, "gather_next", 3))
                for t in both:
                    m = ts(sel_t[:, t, :], con("iota"), rt[:, t, 384:385], op0=ALU.is_equal)
                m.then_inc(S("round_step"), 1)
                dve.wait_ge(S("round_step"), i * 4 + 3)
                for t in both:
                    m = stt(sel[:, t, :], con("iota"), rt[:, t, 385:386], sel_t[:, t, :], ALU.is_equal, ALU.add)
                m.then_inc(S("sel_ready"), 1)
                dve.wait_ge(S("sel_ready"), i + 3)
                ts(rt[:, :, 384:386], rt[:, :, 384:386], -float(P), op0=ALU.add).then_inc(S("round_step"), 1)
                dve.wait_ge(S("round_step"), i * 4 + 4)
            for n in range(4):
                part = slice(2 * n, 2 * n + 2)
                dve.wait_ge(product_ready, base + GROUPS * NPR + n + 1)
                add(xT[:, part, :], xT[:, part, :], quads(bank[n][:, :], 2)).then_inc(free_sem[n], 1)


def constants():
    out = np.zeros((P, NCON), np.float32)
    i = np.arange(P)
    put = lambda name, a: out.__setitem__((slice(None), slice(CON_AT[name][0], CON_AT[name][0] + CON_AT[name][1])), a)
    put("ident", np.eye(P))
    put("upto", i[:, None] <= i[None, :])
    put("before", i[:, None] < i[None, :])
    put("ones", 1.0)
    put("neg_late", np.where(i[:, None] > i[None, :], NEG, 0.0))
    lev = np.zeros((P, LEVELS, P))
    for s in range(LEVELS):
        same = (i[:, None] >> (s + 1)) == (i[None, :] >> (s + 1))
        lev[:, s, :] = same & (((i[None, :] >> s) & 1) == 1) & (((i[:, None] >> s) & 1) == 0)
    put("level", lev.reshape(P, -1))
    half = ROPE // 2
    inv = np.float32(10000.0) ** (-np.arange(half, dtype=np.float32) / np.float32(half))
    a = (np.arange(SEQ, dtype=np.float32)[None, :] * inv[i % half][:, None]).astype(np.float32).astype(np.float64)
    put("rope_cos", np.cos(a))
    put("rope_sin", np.sin(a))
    swap = np.zeros((P, P))
    for t in range(P):
        r = t % ROPE
        swap[t + half if r < half else t - half, t] = -1.0 if r < half else 1.0
    put("swap", swap)
    q, k = i[:, None], np.arange(SEQ)[None, :]
    put("mla_mask", np.concatenate([np.where(k[:, :P] <= q, 0, NEG), np.where(k <= q + P, 0, NEG)], 1))
    put("swa_mask", np.concatenate([np.where(k[:, :P] <= q, 0, NEG),
                                    np.where((k <= q + P) & (q + P - k < 128), 0, NEG)], 1))
    put("iota", i[None, :])
    put("part", i[:, None])
    put("inv_freq", (np.float32(500000.0) ** (-np.arange(0, ROPE2, 2, dtype=np.float32) / np.float32(ROPE2)))[None, :])
    put("eps", EPS)
    return out


def tiles(w, kt, n):
    m = w.shape[1]
    return w.reshape(kt, P, m // n, n).transpose(2, 1, 0, 3).reshape(m // n, P, kt * n)


def by_part(a):
    a = np.atleast_2d(a)
    return a.reshape(a.shape[0], -1, P).transpose(2, 1, 0).reshape(P, -1)


def lay_out(inp):
    g = {k: np.asarray(v) for k, v in inp.items()}
    one = lambda name: g[name][0]
    w_in = one("w_in")
    e = np.cumsum([0, 3072, 1024, 8, 8, 384, 256, 64, 1024, 1024])
    wi = [w_in[:, e[n]:e[n + 1]] for n in range(9)]
    a = {}
    a["x"] = g["x"][0].T.reshape(KD, P, SEQ).transpose(1, 0, 2)
    a["consts"] = constants()
    order = np.stack([np.arange(KF), np.arange(KF) + KF], 1).reshape(-1)
    conv_f = one("conv_ffn_w").reshape(3, 2 * KF, P)[:, order].reshape(3, -1)
    cols = [by_part(one("norm_mix_g")), by_part(one("conv_qkv_w")), by_part(one("gdn_norm_g")),
            by_part(one("mla_q_norm_g")), by_part(one("mla_kv_norm_g")), by_part(one("norm_ffn_g")),
            by_part(conv_f), by_part(g["norm_final_g"]), by_part(one("norm1_g_2")), by_part(one("conv_w_2")),
            by_part(one("conv_b_2")), by_part(one("ssd_norm_g_2")), by_part(one("norm2_g_2"))]
    a["cols"] = np.concatenate(cols, 1)
    rows = [one("gdn_a_log"), one("gdn_dt_bias"), one("dt_bias_2"), one("a_log_2"), one("d_skip_2"),
            one("q_norm_g_2"), one("k_norm_g_2"), one("sinks_2"), one("b_router_group_2"),
            one("b_router_expert_2").reshape(-1)]
    a["rows"] = np.broadcast_to(np.concatenate(rows)[None, :], (P, NROW))
    small = lambda w: w.reshape(KD, P, -1).transpose(1, 0, 2)
    a["w_ab"] = small(np.concatenate([wi[2], wi[3]], 1))
    a["w_lat"] = tiles(np.concatenate([wi[4], wi[5], wi[6], wi[6]], 1), KD, 256)
    a["w_qkv"] = tiles(wi[0], KD, 256)
    a["w_gates"] = tiles(np.concatenate([wi[1], wi[7], wi[8]], 1), KD, 256)
    uq = one("w_uq").reshape(Q_RANK, HEADS, 192)
    a["w_uq"] = tiles(np.concatenate([uq[:, :, :128].reshape(Q_RANK, -1), uq[:, :, 128:].reshape(Q_RANK, -1)], 1),
                      KQ, 512)
    ukv = one("w_ukv").reshape(KV_RANK, HEADS, 256)
    a["w_ukv"] = tiles(np.concatenate([ukv[:, :, :128].reshape(KV_RANK, -1), ukv[:, :, 128:].reshape(KV_RANK, -1)],
                                      1), KKV, 1024)
    a["w_o_gdn"], a["w_o_mla"], a["w_out"] = (tiles(one(n), KD, 256) for n in ("w_o_gdn", "w_o_mla", "w_out"))
    a["w_up"] = tiles(one("w_up").reshape(D, 2 * KF, P)[:, order].reshape(D, -1), KD, 256)
    wd = one("w_down").reshape(2, KF // 2, P, KD, P)
    a["w_down"] = wd.transpose(3, 0, 2, 1, 4).reshape(2 * KD, P, KF // 2 * P)
    w2 = one("w_in_2")
    e = np.cumsum([0, 2048, 3072, 32, 1024, 256, 256, 1024, 1024])
    wi = [w2[:, e[n]:e[n + 1]] for n in range(8)]
    a["w_z2"], a["w_xbc2"], a["w_dt"] = tiles(wi[0], KD, 256), tiles(wi[1], KD, 256), small(wi[2])
    a["w_att2"] = tiles(w2[:, e[3]:e[6]], KD, 256)
    a["w_gates2"] = tiles(w2[:, e[6]:e[8]], KD, 256)
    a["w_ssd_out2"] = tiles(one("w_ssd_out_2"), 16, 128)
    a["w_attn_out2"], a["w_out2"] = tiles(one("w_attn_out_2"), KD, 256), tiles(one("w_out_2"), KD, 256)
    a["w_rt"] = small(np.concatenate([one("w_router_group_2"),
                                      one("w_router_expert_2").transpose(1, 0, 2).reshape(D, EXPERTS)], 1))
    a["pos"] = g["positions_2"][0].reshape(TT, P).T
    for name, kt in (("w_gate_e", KD), ("w_up_e", KD), ("w_down_e", 2)):
        w = one(name + "_2")
        a[name] = w.reshape(EXPERTS, kt, P, -1).transpose(0, 2, 1, 3).reshape(EXPERTS, P, SLOT)
    return {k: np.ascontiguousarray(v) for k, v in a.items()}


def kernel(**inputs):
    import concourse.bacc as bacc
    from concourse.bass_utils import run_bass_kernel_spmd

    arrays = lay_out(inputs)
    nc = bacc.Bacc("TRN2", target_bir_lowering=False, num_devices=1)
    A = {name: nc.dram_tensor(name + "_dram", a.shape, mybir.dt.from_np(a.dtype), kind="ExternalInput").ap()
         for name, a in arrays.items()}
    out = nc.dram_tensor("out_dram", (P, KD, SEQ), F32, kind="ExternalOutput").ap()
    build(nc, A, out)
    r = run_bass_kernel_spmd(nc, [{name + "_dram": a for name, a in arrays.items()}], core_ids=[0])
    got = r.results[0]["out_dram"]
    return got.transpose(2, 1, 0).reshape(1, SEQ, D)
```
